# Optimizing a Trainium2 kernel written in Bass

```python
import math
import jax, jax.numpy as jnp
from jax import lax
import numpy as np

D_MODEL = 1024
BATCH = 1
SEQ = 256
DEPTH = 1

D_MIX = D_MODEL
LRU_WIDTH = D_MIX // 4
LRU_BLOCKS = 4
LRU_CONV = 4
LRU_C = 8.0
HG_HEADS = 4
HG_DK = 64
HG_DV = 64
HG_CHUNK = 64
ATT_HEADS = 8
ATT_HD = 64
MOBA_BLOCK = 256
MOBA_TOPK = 3
Q_BLOCK = 64
D_FF = 4 * D_MODEL
EPS = 1e-6
NEG = -1e30
TINY = 1e-30

SPLITS = (LRU_WIDTH, LRU_WIDTH,
          HG_HEADS * HG_DK, HG_HEADS * HG_DK, HG_HEADS * HG_DV, HG_HEADS * HG_DV,
          ATT_HEADS * ATT_HD, ATT_HEADS * ATT_HD, ATT_HEADS * ATT_HD)
D_IN = sum(SPLITS)
D_OUT_CAT = LRU_WIDTH + HG_HEADS * HG_DV + ATT_HEADS * ATT_HD


def rms_norm(x, g):
    xf = x.astype(jnp.float32)
    y = xf * lax.rsqrt(jnp.mean(xf * xf, axis=-1, keepdims=True) + EPS)
    return (y * g.astype(jnp.float32)).astype(x.dtype)

def rglru_group(xb, yb, conv_w, conv_b, wa, ba, wx, bx, lam):
    Bn, S, W = xb.shape
    xc = lax.conv_general_dilated(
        xb, conv_w.reshape(LRU_CONV, 1, W).astype(xb.dtype), window_strides=(1,),
        padding=[(LRU_CONV - 1, 0)], dimension_numbers=('NWC', 'WIO', 'NWC'),
        feature_group_count=W) + conv_b.astype(xb.dtype)
    xg = xc.reshape(Bn, S, LRU_BLOCKS, W // LRU_BLOCKS)
    r = jax.nn.sigmoid(jnp.einsum('bsgi,gij->bsgj', xg, wa).reshape(Bn, S, W).astype(jnp.float32)
                       + ba.astype(jnp.float32))
    i = jax.nn.sigmoid(jnp.einsum('bsgi,gij->bsgj', xg, wx).reshape(Bn, S, W).astype(jnp.float32)
                       + bx.astype(jnp.float32))
    log_a = -LRU_C * r * jax.nn.softplus(-lam.astype(jnp.float32))
    a = jnp.exp(log_a)
    u = jnp.sqrt(-jnp.expm1(2.0 * log_a)) * (i * xc.astype(jnp.float32))

    def combine(c1, c2):
        a1, b1 = c1
        a2, b2 = c2
        return a1 * a2, a2 * b1 + b2

    _, h = lax.associative_scan(combine, (a, u), axis=1)
    return (h * jax.nn.gelu(yb.astype(jnp.float32))).astype(xb.dtype)

def hgrn2_group(q, f, i, g, lb, norm_w):
    Bn, S, _ = q.shape
    nc = S // HG_CHUNK
    lb = lb.astype(jnp.float32)
    fpre = f.astype(jnp.float32)
    log_f = jnp.logaddexp(jnp.log(jnp.maximum(lb, TINY)), jnp.log1p(-lb) + jax.nn.log_sigmoid(fpre))
    k = (1.0 - lb) * jax.nn.sigmoid(-fpre)
    qs = jax.nn.silu(q.astype(jnp.float32))

    def heads(t, d):
        return t.astype(jnp.float32).reshape(Bn, nc, HG_CHUNK, HG_HEADS, d).transpose(1, 0, 3, 2, 4)

    qh, kh, lfh, vh = heads(qs, HG_DK), heads(k, HG_DK), heads(log_f, HG_DK), heads(i, HG_DV)
    mask = jnp.tril(jnp.ones((HG_CHUNK, HG_CHUNK), dtype=bool))

    def step(state, inp):
        qc, kc, lfc, vc = inp
        b = jnp.cumsum(lfc, axis=2)
        diff = b[:, :, :, None, :] - b[:, :, None, :, :]
        decay = jnp.exp(jnp.where(mask[:, :, None], diff, NEG))
        att = jnp.einsum('bhtd,bhsd,bhtsd->bhts', qc, kc, decay)
        o = jnp.einsum('bhts,bhse->bhte', att, vc) + jnp.einsum('bhtd,bhde->bhte', qc * jnp.exp(b), state)
        b_last = b[:, :, -1:, :]
        new_state = jnp.exp(b_last[:, :, 0, :])[..., None] * state + \
            jnp.einsum('bhsd,bhse->bhde', kc * jnp.exp(b_last - b), vc)
        return new_state, o

    s0 = jnp.zeros((Bn, HG_HEADS, HG_DK, HG_DV), jnp.float32)
    _, o = lax.scan(step, s0, (qh, kh, lfh, vh))
    o = o.transpose(1, 0, 3, 2, 4).reshape(Bn, S, HG_HEADS, HG_DV)
    o = rms_norm(o, norm_w) * jax.nn.silu(g.reshape(Bn, S, HG_HEADS, HG_DV).astype(jnp.float32))
    return o.reshape(Bn, S, HG_HEADS * HG_DV).astype(q.dtype)

def moba_group(cq, ck, cv):
    Bn, S, _ = cq.shape
    H, hd = ATT_HEADS, ATT_HD
    s_pad = -(-S // MOBA_BLOCK) * MOBA_BLOCK
    pad = s_pad - S

    def heads(t):
        t = t.reshape(Bn, S, H, hd).transpose(0, 2, 1, 3)
        return jnp.pad(t, ((0, 0), (0, 0), (0, pad), (0, 0)))

    q, k, v = heads(cq), heads(ck), heads(cv)
    nblk = s_pad // MOBA_BLOCK
    topk = min(MOBA_TOPK, nblk)
    kb = k.reshape(Bn, H, nblk, MOBA_BLOCK, hd)
    vb = v.reshape(Bn, H, nblk, MOBA_BLOCK, hd)
    kmean = jnp.mean(kb.astype(jnp.float32), axis=3).astype(k.dtype)
    scale = 1.0 / math.sqrt(hd)
    slopes = jnp.asarray(2.0 ** (-8.0 * np.arange(1, H + 1) / H), dtype=jnp.float32)
    nq = s_pad // Q_BLOCK
    qs = q.reshape(Bn, H, nq, Q_BLOCK, hd).transpose(2, 0, 1, 3, 4)
    bi = jnp.arange(Bn)[:, None, None, None]
    hi = jnp.arange(H)[None, :, None, None]
    blk_pos = jnp.arange(MOBA_BLOCK)

    def step(args):
        qi, q_blk = args
        t = qi * Q_BLOCK + jnp.arange(Q_BLOCK)
        j = (qi * Q_BLOCK) // MOBA_BLOCK
        gate = jnp.einsum('bhqd,bhnd->bhqn', q_blk, kmean).astype(jnp.float32)
        gate = jnp.where(jnp.arange(nblk) < j, gate, NEG)
        _, sel = lax.top_k(gate, topk)
        valid = jnp.arange(topk) < j
        ksel = kb[bi, hi, sel]
        vsel = vb[bi, hi, sel]
        s_sel = jnp.einsum('bhqd,bhqkld->bhqkl', q_blk, ksel).astype(jnp.float32) * scale
        pos_sel = sel[..., None] * MOBA_BLOCK + blk_pos
        s_sel = s_sel - slopes[:, None, None, None] * (t[:, None, None] - pos_sel).astype(jnp.float32)
        s_sel = jnp.where(valid[:, None], s_sel, NEG)
        k_own = lax.dynamic_slice_in_dim(kb, j, 1, axis=2)[:, :, 0]
        v_own = lax.dynamic_slice_in_dim(vb, j, 1, axis=2)[:, :, 0]
        s_own = jnp.einsum('bhqd,bhld->bhql', q_blk, k_own).astype(jnp.float32) * scale
        rel = t[:, None] - (j * MOBA_BLOCK + blk_pos)[None, :]
        s_own = jnp.where(rel >= 0, s_own - slopes[:, None, None] * rel.astype(jnp.float32), NEG)
        scores = jnp.concatenate([s_own, s_sel.reshape(Bn, H, Q_BLOCK, topk * MOBA_BLOCK)], axis=-1)
        p = jax.nn.softmax(scores, axis=-1).astype(v.dtype)
        p_own = p[..., :MOBA_BLOCK]
        p_sel = p[..., MOBA_BLOCK:].reshape(Bn, H, Q_BLOCK, topk, MOBA_BLOCK)
        out = jnp.einsum('bhql,bhld->bhqd', p_own, v_own) + jnp.einsum('bhqkl,bhqkld->bhqd', p_sel, vsel)
        return out.astype(v.dtype)

    o = lax.map(step, (jnp.arange(nq), qs))
    o = o.transpose(1, 2, 0, 3, 4).reshape(Bn, H, s_pad, hd)[:, :, :S]
    return o.transpose(0, 2, 1, 3).reshape(Bn, S, H * hd)

def first_inputs(seed: int = 0) -> dict:
    key = jax.random.key(seed)
    ks = jax.random.split(key, 20)
    f32 = jnp.float32
    L = DEPTH
    nrm = lambda k, shape, fan: jax.random.normal(k, shape, f32) * (fan ** -0.5)
    gain = lambda k, shape: 1.0 + 0.05 * jax.random.normal(k, shape, f32)
    bw = LRU_WIDTH // LRU_BLOCKS
    u = jax.random.uniform(ks[10], (L, LRU_WIDTH), f32, 0.9, 0.999)
    a_base = u ** (1.0 / LRU_C)
    lam = jnp.log(a_base) - jnp.log1p(-a_base)
    return {
        "x": jax.random.normal(ks[0], (BATCH, SEQ, D_MODEL), f32),
        "w_in": nrm(ks[1], (L, D_MODEL, D_IN), D_MODEL),
        "w_out": nrm(ks[2], (L, D_OUT_CAT, D_MODEL), D_OUT_CAT),
        "norm_mix": gain(ks[3], (L, D_MODEL)),
        "norm_mlp": gain(ks[4], (L, D_MODEL)),
        "lru_conv_w": nrm(ks[5], (L, LRU_CONV, LRU_WIDTH), LRU_CONV),
        "lru_conv_b": 0.01 * jax.random.normal(ks[6], (L, LRU_WIDTH), f32),
        "lru_wa": nrm(ks[7], (L, LRU_BLOCKS, bw, bw), bw),
        "lru_ba": 0.01 * jax.random.normal(ks[8], (L, LRU_WIDTH), f32),
        "lru_wx": nrm(ks[9], (L, LRU_BLOCKS, bw, bw), bw),
        "lru_bx": 0.01 * jax.random.normal(ks[11], (L, LRU_WIDTH), f32),
        "lru_lambda": lam,
        "hg_lower_bounds": 0.1 * jax.random.normal(ks[12], (L, HG_HEADS * HG_DK), f32),
        "hg_norm_w": gain(ks[13], (L, HG_DV)),
        "lru_out_norm": gain(ks[14], (L, LRU_WIDTH)),
        "att_out_norm": gain(ks[15], (L, ATT_HEADS * ATT_HD)),
        "w_ff1": nrm(ks[16], (L, D_MODEL, D_FF), D_MODEL),
        "w_ff2": nrm(ks[17], (L, D_FF, D_MODEL), D_FF),
        "norm_final": gain(ks[18], (D_MODEL,)),
    }

def first_block(x, w_in, w_out, norm_mix, norm_mlp, lru_conv_w, lru_conv_b, lru_wa, lru_ba, lru_wx, lru_bx,
              lru_lambda, hg_lower_bounds, hg_norm_w, lru_out_norm, att_out_norm, w_ff1, w_ff2, norm_final):
    lb_soft = jax.nn.softmax(hg_lower_bounds.astype(jnp.float32), axis=0)
    lower_bounds = jnp.cumsum(lb_soft, axis=0) - lb_soft[0]
    split_at = np.cumsum(SPLITS)[:-1].tolist()
    for l in range(DEPTH):
        h = rms_norm(x, norm_mix[l])
        z = jnp.einsum('bsd,de->bse', h, w_in[l])
        a_x, a_y, b_q, b_f, b_i, b_g, c_q, c_k, c_v = jnp.split(z, split_at, axis=-1)
        ya = rglru_group(a_x, a_y, lru_conv_w[l], lru_conv_b[l], lru_wa[l], lru_ba[l],
                         lru_wx[l], lru_bx[l], lru_lambda[l])
        yb = hgrn2_group(b_q, b_f, b_i, b_g, lower_bounds[l], hg_norm_w[l])
        yc = moba_group(c_q, c_k, c_v)
        y = jnp.concatenate([rms_norm(ya, lru_out_norm[l]), yb.astype(x.dtype),
                             rms_norm(yc, att_out_norm[l])], axis=-1)
        x = x + jnp.einsum('bse,ed->bsd', y, w_out[l])
        h = rms_norm(x, norm_mlp[l])
        u = jnp.square(jax.nn.relu(jnp.einsum('bsd,df->bsf', h, w_ff1[l])))
        x = x + jnp.einsum('bsf,fd->bsd', u, w_ff2[l])
    return rms_norm(x, norm_final)


GLA_HEADS = 4
GLA_DK = 128
GLA_DV = 256
GLA_RANK = 16
GLA_TAU = 16.0
GLA_CHUNK = 64
GLA_QK = GLA_HEADS * GLA_DK
GLA_V = GLA_HEADS * GLA_DV
SGU_GROUPS = 8
SGU_CH = D_MODEL // SGU_GROUPS
SGU_W = SGU_GROUPS * SGU_CH
SGU_CHUNK = 128
PEER_HEADS = 8
PEER_NKEYS = 128
PEER_NEXP = PEER_NKEYS * PEER_NKEYS
PEER_DQ = 256
PEER_TOPK = 16
PEER_BLOCK = 128

IN_SIZES = (GLA_QK, GLA_QK, GLA_V, GLA_V, GLA_RANK, SGU_W, SGU_W, D_MODEL, D_MODEL)
IN_WIDTH = sum(IN_SIZES)
IN_SPLITS = [int(s) for s in np.cumsum(IN_SIZES)[:-1]]


def rms_norm_2(x, w):
    xf = x.astype(jnp.float32)
    y = xf * lax.rsqrt(jnp.mean(xf * xf, axis=-1, keepdims=True) + EPS)
    return (y * w.astype(jnp.float32)).astype(x.dtype)

def layer_norm(x, w, b):
    xf = x.astype(jnp.float32)
    mu = jnp.mean(xf, axis=-1, keepdims=True)
    xc = xf - mu
    y = xc * lax.rsqrt(jnp.mean(xc * xc, axis=-1, keepdims=True) + EPS)
    return (y * w.astype(jnp.float32) + b.astype(jnp.float32)).astype(x.dtype)

def modulate(h, shift, scale):
    return h * (1 + scale[:, None, :]) + shift[:, None, :]

def gla_chunked(q, k, v, log_a):
    B, T, H, dk = q.shape
    dv = v.shape[-1]
    C = GLA_CHUNK
    N = T // C
    f32 = jnp.float32

    def to_chunks(t):
        return t.astype(f32).reshape(B, N, C, H, t.shape[-1]).transpose(1, 0, 3, 2, 4)

    qc, kc, vc, lac = to_chunks(q) * dk ** -0.5, to_chunks(k), to_chunks(v), to_chunks(log_a)
    G = jnp.cumsum(lac, axis=-2)
    G_last = G[..., -1:, :]
    q_dec = qc * jnp.exp(G)
    k_inv = kc * jnp.exp(-G)
    k_tail = kc * jnp.exp(G_last - G)
    mask = jnp.tril(jnp.ones((C, C), dtype=bool))
    A = jnp.where(mask, jnp.einsum('nbhik,nbhjk->nbhij', q_dec, k_inv), 0.0)
    o_intra = jnp.einsum('nbhij,nbhjv->nbhiv', A, vc)

    def step(S, inp):
        qd, kt, vv, gl = inp
        o = jnp.einsum('bhik,bhkv->bhiv', qd, S)
        S = S * jnp.exp(gl)[..., 0, :, None] + jnp.einsum('bhjk,bhjv->bhkv', kt, vv)
        return S, o

    S0 = jnp.zeros((B, H, dk, dv), f32)
    _, o_inter = lax.scan(step, S0, (q_dec, k_tail, vc, G_last))
    o = o_intra + o_inter
    return o.transpose(1, 0, 3, 2, 4).reshape(B, T, H, dv).astype(q.dtype)

def spatial_gating(u, v, w_s, b_s, ln_w, ln_b):
    B, T, _ = v.shape
    N = T // SGU_CHUNK
    v = layer_norm(v, ln_w, ln_b)
    vg = v.reshape(B, N, SGU_CHUNK, SGU_GROUPS, SGU_CH)
    mask = jnp.tril(jnp.ones((SGU_CHUNK, SGU_CHUNK), dtype=bool))
    w = jnp.where(mask[None], w_s, 0)
    s = jnp.einsum('gij,bnjgc->bnigc', w, vg) + b_s.T[None, None, :, :, None]
    return u * s.reshape(B, T, SGU_W)

def peer(h, w_q, keys1, keys2, expert_down, expert_up):
    B, T, D = h.shape
    H, K = PEER_HEADS, PEER_TOPK
    q = jnp.einsum('btd,dq->btq', h, w_q).reshape(B, T, H, 2, PEER_DQ // 2)
    s1 = jnp.einsum('bthc,kc->bthk', q[..., 0, :], keys1).astype(jnp.float32)
    s2 = jnp.einsum('bthc,kc->bthk', q[..., 1, :], keys2).astype(jnp.float32)
    v1, i1 = lax.top_k(s1, K)
    v2, i2 = lax.top_k(s2, K)
    cand = (v1[..., :, None] + v2[..., None, :]).reshape(B, T, H, K * K)
    cidx = (i1[..., :, None] * PEER_NKEYS + i2[..., None, :]).reshape(B, T, H, K * K)
    top_s, pos = lax.top_k(cand, K)
    idx = jnp.take_along_axis(cidx, pos, axis=-1)
    g = jax.nn.softmax(top_s, axis=-1).astype(h.dtype)
    nb = (B * T) // PEER_BLOCK
    xb = h.reshape(nb, PEER_BLOCK, D)
    ib = idx.reshape(nb, PEER_BLOCK, H * K)
    gb = g.reshape(nb, PEER_BLOCK, H * K)

    def block(args):
        xx, ii, gg = args
        u = expert_down[ii]
        a = jax.nn.gelu(jnp.einsum('pd,ped->pe', xx, u), approximate=False)
        vv = expert_up[ii]
        return jnp.einsum('pe,ped->pd', gg * a, vv)

    return lax.map(block, (xb, ib, gb)).reshape(B, T, D)

def second_inputs(seed: int = 0) -> dict:
    key = jax.random.key(seed)
    ks = jax.random.split(key, 24)
    f32 = jnp.float32
    L, D = DEPTH, D_MODEL

    def nrm(k, shape, scale):
        return jax.random.normal(k, shape, f32) * scale

    return {
        'x': nrm(ks[0], (BATCH, SEQ, D), 1.0),
        'c': nrm(ks[1], (BATCH, D), 1.0),
        'w_ada': nrm(ks[2], (L, D, 6 * D), 0.5 * D ** -0.5),
        'b_ada': nrm(ks[3], (L, 6 * D), 0.02),
        'norm1_w': 1.0 + nrm(ks[4], (L, D), 0.02),
        'w_in': nrm(ks[5], (L, D, IN_WIDTH), D ** -0.5),
        'w_alpha_up': nrm(ks[6], (L, GLA_RANK, GLA_QK), GLA_RANK ** -0.5),
        'b_alpha': nrm(ks[7], (L, GLA_QK), 0.1),
        'gla_norm_w': 1.0 + nrm(ks[8], (L, GLA_V), 0.02),
        'sgu_ln_w': 1.0 + nrm(ks[9], (L, SGU_W), 0.02),
        'sgu_ln_b': nrm(ks[10], (L, SGU_W), 0.02),
        'sgu_w': nrm(ks[11], (L, SGU_GROUPS, SGU_CHUNK, SGU_CHUNK), 0.5 * SGU_CHUNK ** -0.5),
        'sgu_b': 1.0 + nrm(ks[12], (L, SGU_GROUPS, SGU_CHUNK), 0.02),
        'w_out': nrm(ks[13], (L, D, D), D ** -0.5),
        'norm2_w': 1.0 + nrm(ks[14], (L, D), 0.02),
        'peer_w_q': nrm(ks[15], (L, D, PEER_HEADS * PEER_DQ), D ** -0.5),
        'peer_keys1': nrm(ks[16], (L, PEER_NKEYS, PEER_DQ // 2), (PEER_DQ // 2) ** -0.5),
        'peer_keys2': nrm(ks[17], (L, PEER_NKEYS, PEER_DQ // 2), (PEER_DQ // 2) ** -0.5),
        'peer_down': nrm(ks[18], (L, PEER_NEXP, D), D ** -0.5),
        'peer_up': nrm(ks[19], (L, PEER_NEXP, D), D ** -0.5),
        'final_norm_w': 1.0 + nrm(ks[20], (D,), 0.02),
    }

def second_block(x, c, w_ada, b_ada, norm1_w, w_in, w_alpha_up, b_alpha, gla_norm_w,
              sgu_ln_w, sgu_ln_b, sgu_w, sgu_b, w_out, norm2_w, peer_w_q, peer_keys1,
              peer_keys2, peer_down, peer_up, final_norm_w):
    B, T, D = x.shape
    silu_c = jax.nn.silu(c)
    for l in range(DEPTH):
        mod = jnp.einsum('bd,de->be', silu_c, w_ada[l]) + b_ada[l]
        shift1, scale1, gate1, shift2, scale2, gate2 = jnp.split(mod, 6, axis=-1)

        h = modulate(rms_norm_2(x, norm1_w[l]), shift1, scale1)
        proj = jnp.einsum('btd,de->bte', h, w_in[l])
        q, k, v, r, a_lr, su, sv, g_a, g_b = jnp.split(proj, IN_SPLITS, axis=-1)

        z = jnp.einsum('btr,rk->btk', a_lr, w_alpha_up[l]) + b_alpha[l]
        log_a = jax.nn.log_sigmoid(z.astype(jnp.float32)) / GLA_TAU
        o = gla_chunked(q.reshape(B, T, GLA_HEADS, GLA_DK), k.reshape(B, T, GLA_HEADS, GLA_DK),
                        v.reshape(B, T, GLA_HEADS, GLA_DV), log_a.reshape(B, T, GLA_HEADS, GLA_DK))
        o = rms_norm_2(o, gla_norm_w[l].reshape(GLA_HEADS, GLA_DV)).reshape(B, T, GLA_V)
        o_gla = o * jax.nn.silu(r)

        o_sgu = spatial_gating(jax.nn.gelu(su, approximate=False), jax.nn.gelu(sv, approximate=False),
                               sgu_w[l], sgu_b[l], sgu_ln_w[l], sgu_ln_b[l])

        merged = jax.nn.sigmoid(g_a) * o_gla + jax.nn.sigmoid(g_b) * o_sgu
        y = jnp.einsum('bte,ed->btd', merged, w_out[l])
        x = x + gate1[:, None, :] * y

        h2 = modulate(rms_norm_2(x, norm2_w[l]), shift2, scale2)
        y2 = peer(h2, peer_w_q[l], peer_keys1[l], peer_keys2[l], peer_down[l], peer_up[l])
        x = x + gate2[:, None, :] * y2
    return rms_norm_2(x, final_norm_w)


def setup_inputs(seed=0):
    out = dict(first_inputs(seed))
    for name, value in second_inputs(seed + 1).items():
        if name != "x":
            out[name + "_2"] = value
    return out


def reference(
    x, w_in, w_out, norm_mix, norm_mlp, lru_conv_w, lru_conv_b, lru_wa, lru_ba, lru_wx, lru_bx,
    lru_lambda, hg_lower_bounds, hg_norm_w, lru_out_norm, att_out_norm, w_ff1, w_ff2,
    norm_final, c_2, w_ada_2, b_ada_2, norm1_w_2, w_in_2, w_alpha_up_2, b_alpha_2, gla_norm_w_2,
    sgu_ln_w_2, sgu_ln_b_2, sgu_w_2, sgu_b_2, w_out_2, norm2_w_2, peer_w_q_2, peer_keys1_2,
    peer_keys2_2, peer_down_2, peer_up_2, final_norm_w_2,
):
    x = first_block(
        x, w_in, w_out, norm_mix, norm_mlp, lru_conv_w, lru_conv_b, lru_wa, lru_ba, lru_wx,
        lru_bx, lru_lambda, hg_lower_bounds, hg_norm_w, lru_out_norm, att_out_norm, w_ff1,
        w_ff2, norm_final,
    )
    return second_block(
        x, c_2, w_ada_2, b_ada_2, norm1_w_2, w_in_2, w_alpha_up_2, b_alpha_2, gla_norm_w_2,
        sgu_ln_w_2, sgu_ln_b_2, sgu_w_2, sgu_b_2, w_out_2, norm2_w_2, peer_w_q_2, peer_keys1_2,
        peer_keys2_2, peer_down_2, peer_up_2, final_norm_w_2,
    )


_drawn_inputs = setup_inputs


def setup_inputs(seed=0):
    import zlib

    import numpy as np

    out = dict(_drawn_inputs(seed))
    spreads = {}
    factors = {'lru_ba': 8.0,
     'lru_bx': 8.0,
     'hg_norm_w': 4.724,
     'lru_out_norm': 2.936,
     'b_ada_2': 4.011,
     'norm1_w_2': 8.0,
     'b_alpha_2': 8.0,
     'gla_norm_w_2': 8.0,
     'sgu_ln_w_2': 8.0,
     'sgu_ln_b_2': 8.0,
     'sgu_b_2': 8.0,
     'norm2_w_2': 8.0,
     'peer_w_q_2': 8.0,
     'peer_keys1_2': 8.0,
     'peer_keys2_2': 8.0,
     'peer_down_2': 8.0,
     'peer_up_2': 8.0,
     'final_norm_w_2': 2.818}
    for name, (base, spread) in spreads.items():
        noise = np.random.default_rng([zlib.crc32(name.encode()), seed]).standard_normal(out[name].shape)
        drawn = base * np.exp(spread * noise) if base else spread * noise
        out[name] = __import__('jax').numpy.asarray(drawn.astype(out[name].dtype))
    for name, factor in factors.items():
        out[name] = (out[name] * factor).astype(out[name].dtype)
    return out
```

```python
import concourse.bass as bass
from concourse import mybir
from concourse.alu_op_type import AluOpType as ALU
from contextlib import ExitStack
import numpy as np

F32 = mybir.dt.float32
F32R = mybir.dt.float32r
U32 = mybir.dt.uint32
ACT = mybir.ActivationFunctionType
AX = mybir.AxisListType

P = 128
D = 1024
T = 256
TT = T // P
KC = D // P
EPS = 1e-6
LOG_TINY = float(np.log(np.float32(1e-30)))
NEXP_ROWS = 128
R = 4

N_IN_F, N_IN_M, N_WOUT, N_FFN, N_IN2_F, N_IN2_M, N_WOUT2, N_WQ, N_PEER = 16, 8, 8, 32, 8, 48, 8, 16, NEXP_ROWS
T_IN_F = 0
T_IN_M = T_IN_F + N_IN_F
T_WOUT = T_IN_M + N_IN_M
T_FFN = T_WOUT + N_WOUT
T_IN2_F = T_FFN + 2 * N_FFN
T_IN2_M = T_IN2_F + N_IN2_F
T_WOUT2 = T_IN2_M + N_IN2_M
T_WQ = T_WOUT2 + N_WOUT2
T_PEER = T_WQ + N_WQ
T_END = T_PEER + 2 * N_PEER
N_ADA = 48

GROUPS = ["mix_T", "in_M", "y_T", "wout", "mlp_T", "ffn", "in2_T", "m_v", "m_r", "m_ga", "m_gb",
          "m_su", "m_sv", "merged_T", "wout2", "wq_T", "peer"]
TRANSPOSES = ["mix_T", "y_T", "mlp_T", "in2_T", "merged_T", "wq_T"]
READ_OUT = {"in_M": "in_m", "wout": "x1_done", "ffn": "x2_done", "m_v": "v_out", "m_r": "r_out",
            "m_ga": "ga_out", "m_gb": "gb_out", "m_su": "su_out", "m_sv": "sv_out", "wout2": "x3_done"}


def acc_freed(group, bank):
    before = GROUPS[:GROUPS.index(group)]
    if not before or group == "peer":
        return None
    last = before[-1]
    return ("turned_xg", turn(last[:-2], 4, bank + 1)) if last in TRANSPOSES else (READ_OUT[last], bank + 1)


def acc_filled(group, bank):
    before = GROUPS[:GROUPS.index(group)]
    return sum(4 if g in TRANSPOSES else 3 for g in before) + bank + 1


COLS = {}
_at = 0
for _name, _n in [("mix", 8), ("mlp", 8), ("n1", 8), ("n2", 8), ("ygain", 8), ("bada", 48), ("c", 8),
                  ("convw", 8), ("convb", 2), ("ba", 2), ("bx", 2), ("lam", 2), ("balpha", 4), ("sgb", 8)]:
    COLS[_name] = (_at, _at + _n)
    _at += _n
NCOLS = _at

LEVELS = [1, 2, 4, 8, 16, 32, 64]
PAIRS = [(a, b) for a in range(16) for b in range(16) if (a + 1) * (b + 1) <= 16]
NPAIR = len(PAIRS)


TURNS = ["mix", "y", "mlp", "in2", "merged", "wq"]
SQUARES = ["mix", "lru", "att", "mlp", "fin", "in2", "sgv", "wq", "last"]
ROOTS = ["mix", "hg", "lru", "att", "mlp", "fin", "in2", "sgv", "gla", "wq", "last"]


def turn(name, per, n):
    return per * TURNS.index(name) + n


def squared(name, n=2):
    return 2 * SQUARES.index(name) + n


def rooted(name):
    return ROOTS.index(name) + 1


class Steps:

    def __init__(self, eng, sem):
        self.eng, self.sem, self.n = eng, sem, 0

    def __call__(self, ins):
        ins.then_inc(self.sem, 1)
        self.n += 1
        return self.n

    def sync(self):
        self.eng.wait_ge(self.sem, self.n)


def build(nc, x, stream, ada, cols, rows, lru_w, hgmask, causal, alibi, iota, walr, wup, sguw, keys, out):
    ctx = ExitStack()
    with ctx:
        def sb(name, shape, dt=F32):
            return ctx.enter_context(nc.sbuf_tensor(name, shape, dt))

        sems = {}

        def S(name):
            if name not in sems:
                sems[name] = ctx.enter_context(nc.semaphore(name))
            return sems[name]

        raw = sb("raw", [P, R, 1024])
        whi = sb("whi", [P, R, 1024], F32R)
        wlo = sb("wlo", [P, R, 1024], F32R)
        xh = sb("xh", [P, KC, T], F32R)
        xl = sb("xl", [P, KC, T], F32R)
        ua = sb("ua", [P, 2, T])
        uh = sb("uh", [P, 2, T], F32R)
        ul = sb("ul", [P, 2, T], F32R)
        xs = sb("xs", [P, TT * D])
        ident = sb("ident", [P, P])
        col = sb("col", [P, NCOLS])
        st = sb("st", [P, 64])
        mod = sb("mod", [P, 48])
        arena = sb("arena", [P, 32768])
        xres = xs[:, :].rearrange("p (a d) -> p a d", a=TT)
        i1T, i2T, gT = (xs[:, 256 * j:256 * (j + 1)] for j in range(3))
        oneA = xs[:, 768:1280].rearrange("p (r n) -> p r n", r=4)
        oneB = xs[:, 1280:1792].rearrange("p (r n) -> p r n", r=4)
        iot = xs[:, 1792:1920]
        x_spill = nc.dram_tensor("x_spill", [P, TT * D], F32, kind="Internal").ap()
        g_spill = nc.dram_tensor("g_spill", [P, D], F32, kind="Internal").ap()

        top = [0]

        def take(n, *dims):
            a = arena[:, top[0]:top[0] + n]
            top[0] += n
            assert top[0] <= 32768, top[0]
            if len(dims) == 2:
                a = a.rearrange("p (a b) -> p a b", a=dims[0])
            if len(dims) == 3:
                a = a.rearrange("p (a b c) -> p a b c", a=dims[0], b=dims[1])
            return a

        xn = take(2048, TT, D)
        xg = take(2048, KC, T)
        tmp = take(1024)
        ones = take(128)
        neghalf = st[:, 48:56]
        shared = top[0]
        zF = take(4096, 16, T)
        zM = take(2048, TT, D)
        y = take(2048, TT, D)
        adar = take(4096, R, 1024)
        lw = take(256, 4, 64)
        sil = take(8)
        c8 = take(2)
        tiny = take(16)
        xc, la, lb_, lc, ld, gy = (take(512, 2, T) for _ in range(6))
        ri = take(1024, 4, T)
        hk, hq, hb, h1, h2 = (take(512, 2, T) for _ in range(5))
        hdec = take(1024, 2, 512)
        hQ = take(1024, 2, 512)
        hK = take(1024, 2, 512)
        sg = take(512, 2, 256)
        att = take(1024, 8, P)
        attx = take(512, 4, P)
        msk = take(1024, 8, P)
        ali = take(384)
        sc, pp, pT = (t_.rearrange("p a b -> p (a b)")[:, 0:768].rearrange("p (a b) -> p a b", a=2)
                      for t_ in (hdec, hQ, hK))
        nmx, psm, prs = take(16), take(16), take(16)
        hss, hrs = take(8), take(8)
        top[0] = shared
        qk = take(2048, 8, T)
        mv, mr, mga, mgb, msu, msv = (take(2048, TT, D) for _ in range(6))
        t1, t2, t3, tG = (take(1024, 4, T) for _ in range(4))
        AT = take(1536, 12, P)
        go = take(2048, TT, D)
        rw = take(3072, 3, D)
        sgw = take(1024, 8, P)
        caus = take(128)
        wal = take(128, KC, 16)
        wupt = t1.rearrange("p a b -> p (a b)")[0:16, 0:512]
        alT = t1.rearrange("p a b -> p (a b)")[0:16, 512:768]
        gss, grs = take(8), take(8)
        gain = take(16)
        dg = mgb.rearrange("p a b -> p (a b)")[:, 0:1024]
        gate1 = take(1024)
        gate2 = tmp
        top[0] = shared
        pq = take(4096, 16, T)
        ky = take(256, 2, P)
        scs = take(4096, 32, P)
        scr = take(4096, 32, P)
        pv = take(512, 32, 16)
        pI = take(512, 32, 16)
        pIf = take(512, 32, 16)
        cand = take(16 * NPAIR, 16, NPAIR)
        cidx = take(16 * NPAIR, 16, NPAIR)
        cand2 = take(16 * NPAIR, 16, NPAIR)
        eqs = take(8 * 16 * NPAIR, 8 * 16, NPAIR)
        tv = take(256, 16, 16)
        tp = take(256, 16, 16)
        tpf = take(256, 16, 16)
        tid = take(256, 16, 16)
        tiu = take(256, 16, 16)
        t1f = take(256, 16, 16)
        t2f = take(256, 16, 16)
        tg = take(256, 16, 16)
        tsm, trs = take(16), take(16)
        G = arena[:, :].rearrange("p (t n) -> p t n", t=T)
        fin_x = arena[:, 0:2048].rearrange("p (a d) -> p a d", a=TT)
        fin_t = arena[:, 2048:4096].rearrange("p (a d) -> p a d", a=TT)
        fin_g = arena[:, 4096:5120]
        fin_w = arena[:, 5120:6144]
        fin_o = arena[:, 6144:8192].rearrange("p (a d) -> p a d", a=TT)

        bank = [ctx.enter_context(nc.psum_tensor(f"bank{i}", [P, 512], F32)) for i in range(8)]

        def c_(name, j=None, n=1):
            a, b = COLS[name]
            return col[:, a:b] if j is None else col[:, a + j:a + j + n]

        def s_(k, n=2):
            return st[:, 2 * k:2 * k + n]

        SS = dict(mix=0, lru=1, att=2, mlp=3, fin=4, n1=5, sgm=6, sgv=7, n2=8, last=9, sgs=10)
        RS_AT = 12

        raw_full = [S(f"raw_full{s}") for s in range(R)]
        ada_full = [S(f"ada_full{s}") for s in range(R)]
        hi_done, lo_done, tile_used = S("hi_done"), S("lo_done"), S("tile_used")
        acc_ready = S("acc_ready")
        ada_used = S("ada_used")

        block = ctx.enter_context(nc.Block())

        @block.sync
        def _(sp):
            def tile(slot, row, free):
                if free is not None:
                    sp.wait_ge(lo_done, free)
                sp.dma_start(raw[:, slot, :], stream[bass.ds(row, P), :]).then_inc(raw_full[slot], 16)

            sp.dma_start(xs[:, :], x).then_inc(S("x_in"), 16)
            sp.dma_start(col[:, :], cols).then_inc(S("col_in"), 16)
            sp.dma_start(ident[:, :], iota[:, P:2 * P]).then_inc(S("ident_in"), 16)
            for n in range(R):
                tile(n, n * P, None)
            sp.dma_start(lw.rearrange("p a b -> p (a b)"), lru_w).then_inc(S("consts1_in"), 16)
            sp.dma_start(msk.rearrange("p a b -> p (a b)").bitcast(U32), hgmask).then_inc(S("consts1_in"), 16)
            sp.dma_start(tmp, rows[:, 0:D].to_broadcast([P, D])).then_inc(S("consts1_in"), 16)
            sp.dma_start(ali, alibi).then_inc(S("consts1_in"), 16)
            with sp.Fori(0, (T_FFN - R) // R) as i:
                for u in range(R):
                    tile(u, i * (R * P) + (R + u) * P, i * R + (u + 1))
            for n in range(R):
                sp.dma_start(adar[:, n, :], ada[n * P:(n + 1) * P, :]).then_inc(ada_full[n], 16)
            with sp.Fori(0, N_ADA // R - 1) as i:
                for u in range(R):
                    sp.wait_ge(ada_used, i * R + (u + 1))
                    sp.dma_start(adar[:, u, :], ada[bass.ds(i * (R * P) + (R + u) * P, P), :])\
                        .then_inc(ada_full[u], 16)
            with sp.Fori(0, (T_IN2_F + 8 - T_FFN) // R) as i:
                for u in range(R):
                    tile(u, i * (R * P) + (T_FFN + u) * P, i * R + (T_FFN - R + u + 1))
            sp.wait_ge(S("fin_done"), 2)
            sp.dma_start(wal.rearrange("p a b -> p (a b)"), walr).then_inc(S("consts2_in"), 16)
            sp.dma_start(wupt, wup).then_inc(S("consts2_in"), 16)
            sp.dma_start(rw.rearrange("p a b -> p (a b)"), rows[:, D:4 * D].to_broadcast([P, 3 * D]))\
                .then_inc(S("consts2_in"), 16)
            sp.dma_start(sgw.rearrange("p a b -> p (a b)"), sguw).then_inc(S("consts2_in"), 16)
            sp.dma_start(caus, causal).then_inc(S("consts2_in"), 16)
            with sp.Fori(0, (T_WQ - T_IN2_F) // R) as i:
                for u in range(R):
                    tile(u, i * (R * P) + (T_IN2_F + 8 + u) * P, i * R + (T_IN2_F + 8 - R + u + 1))
            sp.wait_ge(S("unturned"), turn("wq", 2, 2))
            sp.dma_start(x_spill, xs[:, :]).then_inc(S("spilled"), 16)
            sp.wait_ge(S("gates_done"), 4)
            sp.dma_start(g_spill, gate2).then_inc(S("spilled"), 16)
            sp.wait_ge(S("spilled"), 32)
            sp.dma_start(iot, iota[:, 0:P]).then_inc(S("iota_in"), 16)
            sp.wait_ge(S("turned_lo"), turn("wq", 4, 4))
            sp.dma_start(ky.rearrange("p a b -> p (a b)"), keys).then_inc(S("keys_in"), 16)
            with sp.Fori(0, (T_END - T_WQ - 8) // R) as i:
                for u in range(R):
                    tile(u, i * (R * P) + (T_WQ + 8 + u) * P, i * R + (T_WQ + 8 - R + u + 1))
            sp.wait_ge(S("peer_gated"), N_PEER)
            sp.dma_start(fin_x.rearrange("p a d -> p (a d)"), x_spill).then_inc(S("last_in"), 16)
            sp.dma_start(fin_g, g_spill).then_inc(S("last_in"), 16)
            sp.dma_start(fin_w, rows[:, 4 * D:5 * D].to_broadcast([P, D])).then_inc(S("last_in"), 16)
            for tt in range(TT):
                sp.wait_ge(S("out_done"), tt + 1)
                sp.dma_start(out[tt * P:(tt + 1) * P, :], fin_o[:, tt, :]).then_inc(S("stored"), 16)
            sp.wait_ge(S("stored"), 16 * TT)

        @block.gpsimd
        def _(pool):
            def lo(slot, count):
                pool.wait_ge(hi_done, count)
                nc.gpsimd.tensor_tensor(wlo[:, slot, :], raw[:, slot, :], whi[:, slot, :].bitcast(F32),
                                        ALU.subtract).then_inc(lo_done, 1)

            def los(a, b):
                with pool.Fori(0, (b - a) // R) as i:
                    for u in range(R):
                        lo((a + u) % R, i * R + (a + u + 1))

            own = Steps(pool, S("pool_steps"))

            def rstd(sem, count, src, dst, n, scale, done):
                pool.wait_ge(sem, count)
                own(nc.gpsimd.tensor_scalar(dst, src, scale, EPS, ALU.mult, ALU.add))
                own.sync()
                nc.gpsimd.tensor_tensor(dst, dst, neghalf[:, 0:n], ALU.pow).then_inc(done, 1)

            def rs(name):
                return st[:, 2 * (RS_AT + SS[name]):2 * (RS_AT + SS[name]) + 2]

            own(nc.gpsimd.memset(neghalf, -0.5))
            nc.gpsimd.memset(ones, 1.0).then_inc(S("ones_set"), 1)
            own.sync()
            rstd(S("squares"), squared("mix"), s_(SS["mix"]), rs("mix"), 2, 1.0 / D, S("roots"))
            for n in range(R):
                lo(n, n + 1)
            los(R, T_WOUT + R)
            rstd(S("hg_ss"), 1, hss, hrs, 8, 1.0 / 64, S("roots"))
            rstd(S("squares"), squared("lru"), s_(SS["lru"]), rs("lru"), 2, 1.0 / 256, S("roots"))
            rstd(S("squares"), squared("att"), s_(SS["att"]), rs("att"), 2, 1.0 / 512, S("roots"))
            los(T_WOUT + R, T_FFN + R)
            rstd(S("squares"), squared("mlp"), s_(SS["mlp"]), rs("mlp"), 2, 1.0 / D, S("roots"))
            los(T_FFN + R, T_IN2_F + R)
            rstd(S("squares"), squared("fin"), s_(SS["fin"]), rs("fin"), 2, 1.0 / D, S("roots"))
            rstd(S("squares"), squared("in2"), s_(SS["n1"]), rs("n1"), 2, 1.0 / D, S("roots"))
            los(T_IN2_F + R, T_WOUT2 + R)
            rstd(S("squares"), squared("sgv"), s_(SS["sgv"]), rs("sgv"), 2, 1.0 / D, S("roots"))
            rstd(S("gla_ss"), 8, gss, grs, 8, 1.0 / 256, S("roots"))
            los(T_WOUT2 + R, T_WQ + R)
            rstd(S("squares"), squared("wq"), s_(SS["n2"]), rs("n2"), 2, 1.0 / D, S("roots"))
            los(T_WQ + R, T_END)
            rstd(S("squares"), squared("last"), s_(SS["last"]), rs("last"), 2, 1.0 / D, S("roots"))

        @block.scalar
        def _(act):
            def hi(slot, group, used):
                act.wait_ge(raw_full[slot], group * 16 + 16)
                if used is not None:
                    act.wait_ge(tile_used, used)
                nc.scalar.activation(whi[:, slot, :], raw[:, slot, :], ACT.Copy).then_inc(hi_done, 1)

            def his(a, b):
                with act.Fori(0, (b - a) // R) as i:
                    for u in range(R):
                        hi((a + u) % R, i + (a + u) // R, i * R + (a + u + 1 - R))

            own = Steps(act, S("act_steps"))

            def sums(src, tt, n, scratch, dst, done):
                nc.scalar.activation(scratch[:, tt, 0:n], src, ACT.Square, accum_out=dst[:, tt:tt + 1])\
                    .then_inc(done, 1)

            def upper(name):
                for b in range(4):
                    act.wait_ge(S("turned_xg"), turn(name, 4, b + 1))
                    nc.scalar.activation(xh[:, 2 * b:2 * b + 2, :], xg[:, 2 * b:2 * b + 2, :], ACT.Copy)\
                        .then_inc(S("turned_hi"), 1)

            act.wait_ge(S("x_in"), 16)
            for tt in range(TT):
                sums(xres[:, tt, :], tt, D, xn, s_(SS["mix"]), S("squares"))
            for n in range(R):
                hi(n, 0, None)
            act.wait_ge(S("col_in"), 16)
            nc.scalar.activation(sil, c_("c"), ACT.Sigmoid).then_inc(S("sil_sig"), 1)
            act.wait_ge(S("lam_abs"), 1)
            nc.scalar.activation(tiny[:, 0:2], tiny[:, 0:2], ACT.Exp, scale=-1.0).then_inc(S("lam_exp"), 1)
            upper("mix")
            his(R, T_WOUT + R)

            act.wait_ge(S("in_f"), 16)
            nc.scalar.activation(hk, zF[:, 6:8, :], ACT.Sigmoid, scale=-1.0).then_inc(S("hk_done"), 1)
            nc.scalar.activation(hq, zF[:, 4:6, :], ACT.Sigmoid).then_inc(S("hq_sig"), 1)
            act.wait_ge(S("in_m"), 4)
            nc.scalar.activation(sg, zM[:, :, 256:512], ACT.Sigmoid).then_inc(S("sg_sig"), 1)
            act.wait_ge(S("gy_arg"), 1)
            nc.scalar.activation(ld, gy, ACT.Sigmoid, scale=2.0 * 0.7978845608028654).then_inc(S("gy_sig"), 1)
            act.wait_ge(S("lru_gates"), 1)
            for c in range(2):
                nc.scalar.activation(ri[:, c, :], bank[6][:, c * T:(c + 1) * T], ACT.Sigmoid, bias=c_("ba", c))
            for c in range(2):
                last = nc.scalar.activation(ri[:, 2 + c, :], bank[7][:, c * T:(c + 1) * T], ACT.Sigmoid,
                                            bias=c_("bx", c))
            last.then_inc(S("ri_done"), 1)
            for k, src in enumerate((h1, h2)):
                act.wait_ge(S("hf_abs"), k + 1)
                own(nc.scalar.activation(src, src, ACT.Exp, scale=-1.0))
                own.sync()
                nc.scalar.activation(src, src, ACT.Ln, bias=1.0).then_inc(S("hf_ln"), 1)
            for l, h in enumerate(LEVELS):
                act.wait_ge(S("h_diff"), l + 1)
                d = hdec[:, l % 2, :].rearrange("p (a two h) -> p a two h", two=2, h=h)
                nc.scalar.activation(d[:, :, 0, :], d[:, :, 0, :], ACT.Exp, scale=-1.0)
                nc.scalar.activation(d[:, :, 1, :], d[:, :, 1, :], ACT.Exp).then_inc(S("h_dec"), 1)
            act.wait_ge(S("h_diff"), 8)
            nc.scalar.activation(hdec[:, 1, 0:256], hdec[:, 1, 0:256], ACT.Exp, scale=-1.0)
            nc.scalar.activation(hdec[:, 1, 256:512].rearrange("p (c t) -> p c t", c=2), hb[:, :, P:T],
                                 ACT.Exp).then_inc(S("h_dec"), 1)
            act.wait_ge(S("la_done"), 1)
            nc.scalar.activation(lb_, la, ACT.Exp)
            nc.scalar.activation(lc, la, ACT.Tanh).then_inc(S("a_done"), 1)
            for h in range(8):
                act.wait_ge(S("a_max"), h + 1)
                if h >= 2:
                    act.wait_ge(S("a_tr"), h - 1)
                for tt, (a, b) in enumerate(((0, 128), (128, 384))):
                    last = nc.scalar.activation(pp[:, h % 2, a:b], sc[:, h % 2, a:b], ACT.Exp,
                                                bias=nmx[:, 2 * h + tt:2 * h + tt + 1],
                                                accum_out=psm[:, 2 * h + tt:2 * h + tt + 1])
                last.then_inc(S("a_exp"), 1)
            act.wait_ge(S("lru_m2"), 1)
            nc.scalar.activation(lc, lc, ACT.Sqrt, scale=-1.0).then_inc(S("lru_sqrt"), 1)
            for tt in range(TT):
                act.wait_ge(S("lru_y"), 1)
                sums(y[:, tt, 0:256], tt, 256, xn, s_(SS["lru"]), S("squares"))
            act.wait_ge(S("att_y"), 2)
            act.wait_ge(S("squares"), squared("lru"))
            for tt in range(TT):
                sums(y[:, tt, 512:1024], tt, 512, xn, s_(SS["att"]), S("squares"))
            upper("y")
            his(T_WOUT + R, T_FFN + R)

            act.wait_ge(S("x1_done"), 4)
            for tt in range(TT):
                sums(xres[:, tt, :], tt, D, xn, s_(SS["mlp"]), S("squares"))
            upper("mlp")

            def unit(slot, used, freed, func, done):
                act.wait_ge(tile_used, used)
                if freed is not None:
                    act.wait_ge(S(done + "_lo"), freed)
                nc.scalar.activation(ua[:, slot, :], bank[4 + slot][:, 0:T], func).then_inc(S(done + "_act"), 1)

            def units(base, count, func, name, ahead):
                def his_of(i, n0):
                    for n in (base + 3 + n0 * 2, base + 4 + n0 * 2):
                        if ahead or n < T_END:
                            hi(n % R, i + n // R if i is not None else n // R,
                               i * R + (n + 1 - R) if i is not None else n + 1 - R)

                unit(0, base + 1, None, func, name)
                hi((base + 4) % R, (base + 4) // R, base + 1)
                unit(1, base + 2, None, func, name)
                his_of(None, 1)
                looped = (count - 2) // 2 if ahead else (count - 2) // 2 - 1
                with act.Fori(0, looped) as j:
                    for u in range(2):
                        unit(u, j * 4 + (base + 4 + 2 * u), j * 2 + (u + 1), func, name)
                        his_of(j, 2 + u)
                for i in range(2 + 2 * looped, count):
                    unit(i % 2, base + 2 * i, i - 1, func, name)
                    his_of(None, i)
                if ahead:
                    n = base + 2 * count + 3
                    hi(n % R, n // R, n + 1 - R)

            units(T_FFN, N_FFN, ACT.Relu, "ffn", True)

            act.wait_ge(S("x2_done"), 4)
            for tt in range(TT):
                sums(xres[:, tt, :], tt, D, xn, s_(SS["fin"]), S("squares"))
            act.wait_ge(S("fin_done"), 2)
            act.wait_ge(S("squares"), squared("fin"))
            for tt in range(TT):
                sums(xres[:, tt, :], tt, D, xn, s_(SS["n1"]), S("squares"))
            upper("in2")
            his(T_IN2_F + R, T_IN2_M + 8 + R)
            act.wait_ge(S("z_abs"), 1)
            own(nc.scalar.activation(t1, t1, ACT.Exp, scale=-1.0))
            own.sync()
            nc.scalar.activation(t1, t1, ACT.Ln, bias=1.0).then_inc(S("z_ln"), 1)
            his(T_IN2_M + 8 + R, T_IN2_M + 16 + R)
            act.wait_ge(S("g_diff"), 1)
            nc.scalar.activation(t2, t1, ACT.Exp, scale=1.0 / 16)
            nc.scalar.activation(t3, t1, ACT.Exp, scale=-1.0 / 16).then_inc(S("g_dec"), 1)
            act.wait_ge(S("g_diffx"), 1)
            nc.scalar.activation(t1[:, :, 0:P], t1[:, :, 0:P], ACT.Exp, scale=-1.0 / 16)
            nc.scalar.activation(t1[:, :, P:T], tG[:, :, P:T], ACT.Exp, scale=1.0 / 16).then_inc(S("g_dec"), 1)
            act.wait_ge(S("r_out"), 4)
            nc.scalar.activation(xn, mr, ACT.Sigmoid).then_inc(S("r_sig"), 1)

            def read_out(group, tiles_end, dst, func, sum_to=None):
                for b in range(4):
                    if b < 3:
                        act.wait_ge(acc_ready, acc_filled(group, b))
                    else:
                        act.wait_ge(tile_used, tiles_end)
                    extra = {} if sum_to is None else dict(accum_out=sum_to[:, b:b + 1])
                    last = nc.scalar.activation(dst[:, b // 2, (b % 2) * 512:(b % 2 + 1) * 512], bank[b][:, :],
                                                func, **extra)
                    last.then_inc(S(READ_OUT[group]), 1)

            for j, (group, dst, func) in enumerate((("m_ga", mga, ACT.Sigmoid), ("m_gb", mgb, ACT.Sigmoid),
                                                    ("m_su", msu, ACT.Gelu), ("m_sv", msv, ACT.Gelu))):
                a = T_IN2_M + 16 + 8 * j
                if group == "m_gb":
                    act.wait_ge(S("gates_done"), 4)
                his(a + R, a + 8 + R)
                read_out(group, a + 8, dst, func, st[:, 2 * SS["sgs"]:2 * SS["sgs"] + 4] if group == "m_sv" else None)
            act.wait_ge(S("sg_mean"), 1)
            act.wait_ge(S("r_gated"), 1)
            for tt in range(TT):
                nc.scalar.activation(xn[:, tt, :], msv[:, tt, :], ACT.Square, bias=s_(SS["sgm"])[:, tt:tt + 1],
                                     accum_out=s_(SS["sgv"])[:, tt:tt + 1]).then_inc(S("squares"), 1)
            act.wait_ge(S("squares"), squared("sgv"))
            act.wait_ge(S("gla_o"), 1)
            for tt in range(TT):
                for h in range(4):
                    nc.scalar.activation(xn[:, tt, h * T:(h + 1) * T],
                                         bank[4 + 2 * tt + h // 2][:, (h % 2) * T:(h % 2 + 1) * T], ACT.Square,
                                         accum_out=gss[:, 4 * tt + h:4 * tt + h + 1]).then_inc(S("gla_ss"), 1)
            upper("merged")
            his(T_WOUT2 + R, T_WQ + R)
            act.wait_ge(S("x3_done"), 4)
            for tt in range(TT):
                sums(xres[:, tt, :], tt, D, xn, s_(SS["n2"]), S("squares"))
            upper("wq")
            his(T_WQ + R, T_PEER + R)
            act.wait_ge(S("top_shift"), 1)
            nc.scalar.activation(tg, tg, ACT.Exp).then_inc(S("top_exp"), 1)
            with act.Fori(0, T // 8) as i:
                for b in range(2):
                    act.wait_ge(S("onehot_used"), i * 8 + (4 * b + 4))
                    nc.scalar.activation(arena[:, bass.ds(i * 1024 + 512 * b, 512)], bank[b][:, :], ACT.Copy)\
                        .then_inc(S(f"g_copied{b}"), 1)
            units(T_PEER, N_PEER, ACT.Gelu, "peer", False)
            act.wait_ge(S("x4_done"), 4)
            for tt in range(TT):
                sums(fin_x[:, tt, :], tt, D, fin_o, s_(SS["last"]), S("squares"))

        @block.tensor
        def _(pe):
            def f_tile(slot, count, dst):
                pe.wait_ge(lo_done, count)
                for k in range(KC):
                    h_, l_ = whi[:, slot, k * P:(k + 1) * P], wlo[:, slot, k * P:(k + 1) * P]
                    nc.tensor.matmul(dst, h_, xh[:, k, :], start=(k == 0), stop=False)
                    nc.tensor.matmul(dst, h_, xl[:, k, :], start=False, stop=False)
                    last = nc.tensor.matmul(dst, l_, xh[:, k, :], start=False, stop=(k == KC - 1))
                last.then_inc(tile_used, 1)

            def m_tile(slot, count, ah, al, group=None, final=False):
                pe.wait_ge(lo_done, count)
                for b in range(4):
                    tt, half = b // 2, b % 2
                    cs = slice(half * 512, (half + 1) * 512)
                    ts = slice(tt * P, (tt + 1) * P)
                    if group is not None and acc_freed(group, b):
                        name, n = acc_freed(group, b)
                        pe.wait_ge(S(name), n)
                    nc.tensor.matmul(bank[b][:, :], ah[:, ts], whi[:, slot, cs], start=group is not None, stop=False)
                    nc.tensor.matmul(bank[b][:, :], ah[:, ts], wlo[:, slot, cs], start=False, stop=False)
                    last = nc.tensor.matmul(bank[b][:, :], al[:, ts], whi[:, slot, cs], start=False, stop=final)
                    if b == 3:
                        last.then_inc(tile_used, 1)
                    elif final:
                        last.then_inc(acc_ready, 1)

            def m_group(a, group):
                for k in range(KC):
                    m_tile((a + k) % R, a + k + 1, xh[:, k, :], xl[:, k, :], group if k == 0 else None, k == KC - 1)

            def transposes(group, name, src):
                pe.wait_ge(S("unturned"), turn(name, 2, 2))
                for b in range(4):
                    freed = acc_freed(group, b)
                    if freed:
                        pe.wait_ge(S(freed[0]), freed[1])
                    for j in range(2):
                        for tt in range(TT):
                            k = 2 * b + j
                            last = nc.tensor.transpose(bank[b][:, j * T + tt * P:j * T + (tt + 1) * P],
                                                       src[:, tt, k * P:(k + 1) * P], ident[:, :])
                    last.then_inc(acc_ready, 1)

            pe.wait_ge(S("ident_in"), 16)
            transposes("mix_T", "mix", xn)
            pe.wait_ge(S("turned_lo"), turn("mix", 4, 4))
            for n in range(2):
                f_tile(n, n + 1, bank[4 + n][:, 0:T])
            for n in range(2, R):
                pe.wait_ge(S("in_f"), n - 1)
                f_tile(n, n + 1, bank[4 + n % 2][:, 0:T])
            with pe.Fori(0, N_IN_F // R - 1) as i:
                for u in range(R):
                    pe.wait_ge(S("in_f"), i * R + (R + u - 1))
                    f_tile(u, i * R + (R + u + 1), bank[4 + u % 2][:, 0:T])
            m_group(T_IN_M, "in_M")

            pe.wait_ge(S("consts1_in"), 64)
            pe.wait_ge(S("xc_done"), 1)
            for g in range(2):
                for c in range(2):
                    for b in range(2):
                        ps = slice(64 * b, 64 * b + 64)
                        last = nc.tensor.matmul(bank[6 + g][ps, c * T:(c + 1) * T], lw[ps, 2 * g + c, :],
                                                xc[ps, c, :], start=True, stop=True)
            last.then_inc(S("lru_gates"), 1)

            def ada_tiles(a, b):
                with pe.Fori(a // R, b // R) as i:
                    for u in range(R):
                        pe.wait_ge(ada_full[u], i * 16 + 16)
                        for k in range(KC):
                            last = nc.tensor.matmul(bank[3][:, bass.ds(i * R + u, 1)],
                                                    adar[:, u, k * P:(k + 1) * P], sil[:, k:k + 1],
                                                    start=(k == 0), stop=(k == KC - 1))
                        last.then_inc(ada_used, 1)

            pe.wait_ge(S("in_m"), 4)
            pe.wait_ge(S("sil_done"), 1)
            ada_tiles(0, 16)

            for l in range(8):
                pe.wait_ge(S("h_qk"), l + 1)
                src_k, src_q = (hK[:, (l - 1) % 2, :], hQ[:, (l - 1) % 2, :]) if l else \
                    (hk.rearrange("p a b -> p (a b)"), hq.rearrange("p a b -> p (a b)"))
                if l == 0:
                    pe.wait_ge(S("ri_done"), 1)
                if l >= 2:
                    pe.wait_ge(S("h_acc"), 2 * (l - 1))
                for n in range(4):
                    tt, c = n // 2, n % 2
                    for odd in range(2):
                        ps = slice(64 * odd, 64 * odd + 64)
                        cs = slice(c * T + tt * P, c * T + (tt + 1) * P)
                        last = nc.tensor.matmul(bank[4 + 2 * (l % 2) + odd][:, n * P:(n + 1) * P], src_k[ps, cs],
                                                src_q[ps, cs], start=True, stop=True)
                        if n == 3:
                            last.then_inc(S("h_sc"), 1)
            pe.wait_ge(S("h_qk"), 9)
            pe.wait_ge(S("h_acc"), 14)
            for c in range(2):
                for odd in range(2):
                    ps = slice(64 * odd, 64 * odd + 64)
                    cs = slice(c * P, (c + 1) * P)
                    last = nc.tensor.matmul(bank[4 + odd][:, cs], hdec[ps, 1, 0:256][:, cs],
                                            hdec[ps, 1, 256:512][:, cs], start=True, stop=True)
                    if c:
                        last.then_inc(S("h_sc"), 1)
            pe.wait_ge(S("h_acc"), 18)
            for tt in range(TT):
                for h in range(4):
                    dst = bank[6][:, tt * T + h * 64:tt * T + (h + 1) * 64]
                    last = nc.tensor.matmul(dst, att[:, 4 * (h % 2) + 2 * tt + h // 2, :], zM[:, tt, h * 64:(h + 1) * 64],
                                            start=True, stop=(tt == 0))
                    if tt:
                        last = nc.tensor.matmul(dst, attx[:, 2 * (h % 2) + h // 2, :], zM[:, 0, h * 64:(h + 1) * 64],
                                                start=False, stop=True)
            last.then_inc(S("h_o"), 1)
            ada_tiles(16, 32)

            def a_scores(h):
                ps = slice(64 * (h % 2), 64 * (h % 2) + 64)
                if h >= 2:
                    pe.wait_ge(S("a_max"), h - 1)
                q_, k_ = zF[ps, 8 + h // 2, :], zF[ps, 12 + h // 2, :]
                nc.tensor.matmul(bank[6 + h % 2][:, 0:128], q_[:, 0:P], k_[:, 0:P], start=True, stop=True)
                nc.tensor.matmul(bank[6 + h % 2][:, 128:384], q_[:, P:T], k_, start=True, stop=True)\
                    .then_inc(S("a_sc"), 1)

            pe.wait_ge(S("hg_y"), 1)
            a_scores(0)
            a_scores(1)
            for h in range(8):
                pe.wait_ge(S("a_exp"), h + 1)
                if h >= 2:
                    pe.wait_ge(S("a_pT"), h - 1)
                for j in range(3):
                    last = nc.tensor.transpose(bank[4 + h % 2][:, j * P:(j + 1) * P], pp[:, h % 2, j * P:(j + 1) * P],
                                               ident[:, :])
                last.then_inc(S("a_tr"), 1)
                if h + 2 < 8:
                    a_scores(h + 2)
                pe.wait_ge(S("a_pT"), h + 1)
                v_ = slice(512 + 64 * h, 512 + 64 * h + 64)
                o_ = slice(64 * h, 64 * h + 64)
                nc.tensor.matmul(bank[0][:, o_], pT[:, h % 2, 0:128], zM[:, 0, v_], start=True, stop=True)
                nc.tensor.matmul(bank[1][:, o_], pT[:, h % 2, 128:256], zM[:, 0, v_], start=True, stop=False)
                nc.tensor.matmul(bank[1][:, o_], pT[:, h % 2, 256:384], zM[:, 1, v_], start=False, stop=True)\
                    .then_inc(S("a_o"), 1)
            pe.wait_ge(S("lru_h"), 1)
            for tt in range(TT):
                for c in range(2):
                    last = nc.tensor.transpose(bank[6][:, tt * T + c * P:tt * T + (c + 1) * P],
                                               xc[:, c, tt * P:(tt + 1) * P], ident[:, :])
            last.then_inc(S("lru_tr"), 1)
            ada_tiles(32, 48)
            pe.wait_ge(S("att_y"), 2)
            pe.wait_ge(S("mod_done"), 1)
            transposes("y_T", "y", y)
            pe.wait_ge(S("turned_lo"), turn("y", 4, 4))
            m_group(T_WOUT, "wout")

            transposes("mlp_T", "mlp", xn)
            pe.wait_ge(S("turned_lo"), turn("mlp", 4, 4))

            def pairs(base, count, group, name):
                def m_of(slot, count_, u, ready, **kw):
                    pe.wait_ge(S(name + "_lo"), ready)
                    m_tile(slot, count_, uh[:, u, :], ul[:, u, :], **kw)

                f_tile(base % R, base + 1, bank[4][:, 0:T])
                f_tile((base + 1) % R, base + 2, bank[5][:, 0:T])
                m_of((base + 2) % R, base + 3, 0, 1, group=group)
                with pe.Fori(0, (count - 2) // 2) as j:
                    for u in range(2):
                        pe.wait_ge(S(name + "_act"), j * 2 + (1 + u))
                        f_tile((base + 3 + 2 * u) % R, j * 4 + (base + 4 + 2 * u), bank[4 + u][:, 0:T])
                        m_of((base + 4 + 2 * u) % R, j * 4 + (base + 5 + 2 * u), (1 + u) % 2, j * 2 + (2 + u))
                n = base + 2 * count - 1
                m_of(n % R, n + 1, (count - 1) % 2, count, final=True)

            pairs(T_FFN, N_FFN, "ffn", "ffn")

            transposes("in2_T", "in2", xn)
            pe.wait_ge(S("turned_lo"), turn("in2", 4, 4))
            for n in range(2):
                f_tile((T_IN2_F + n) % R, T_IN2_F + n + 1, bank[4 + n][:, 0:T])
            for n in range(2, N_IN2_F):
                pe.wait_ge(S("qk_out"), n - 1)
                f_tile((T_IN2_F + n) % R, T_IN2_F + n + 1, bank[4 + n % 2][:, 0:T])
            pe.wait_ge(S("consts2_in"), 80)
            for k in range(KC):
                last = nc.tensor.matmul(bank[6][0:16, 0:T], wal[:, k, :], xg[:, k, :], start=(k == 0),
                                        stop=(k == KC - 1))
            last.then_inc(S("alr"), 1)
            m_group(T_IN2_M, "m_v")
            pe.wait_ge(S("alr_out"), 1)
            pe.wait_ge(S("consts2_in"), 80)
            for h in range(4):
                last = nc.tensor.matmul(bank[6 + h // 2][:, (h % 2) * T:(h % 2 + 1) * T], wupt[:, h * P:(h + 1) * P],
                                        alT, start=True, stop=True)
            last.then_inc(S("z_mm"), 1)
            m_group(T_IN2_M + 8, "m_r")
            for g in range(2):
                pe.wait_ge(S("diag"), g + 1)
                if g:
                    pe.wait_ge(S("gates_done"), 2)
                for k in range(KC):
                    last = nc.tensor.matmul(bank[4 + k // 4][:, (k % 4) * P:(k % 4 + 1) * P], ones, dg[:, k * P:(k + 1) * P],
                                            start=True, stop=True)
                    if k % 4 == 3:
                        last.then_inc(S("gate_mm"), 1)
            m_group(T_IN2_M + 16, "m_ga")
            pe.wait_ge(S("g_qk"), 2)
            pe.wait_ge(S("gates_done"), 4)
            for tt in range(TT):
                for h in range(4):
                    last = nc.tensor.matmul(bank[4 + tt][:, h * P:(h + 1) * P], t3[:, h, tt * P:(tt + 1) * P],
                                            t2[:, h, tt * P:(tt + 1) * P], start=True, stop=True)
                last.then_inc(S("g_sc"), 1)
            for h in range(4):
                last = nc.tensor.matmul(bank[6][:, h * P:(h + 1) * P], t1[:, h, 0:P], t1[:, h, P:T],
                                        start=True, stop=True)
            last.then_inc(S("g_sc"), 1)
            m_group(T_IN2_M + 24, "m_gb")
            m_group(T_IN2_M + 32, "m_su")
            m_group(T_IN2_M + 40, "m_sv")
            pe.wait_ge(S("g_at"), 3)
            for tt in range(TT):
                for h in range(4):
                    dst = bank[4 + 2 * tt + h // 2][:, (h % 2) * T:(h % 2 + 1) * T]
                    last = nc.tensor.matmul(dst, AT[:, 4 * tt + h, :], mv[:, tt, h * T:(h + 1) * T],
                                            start=True, stop=(tt == 0))
                    if tt:
                        last = nc.tensor.matmul(dst, AT[:, 8 + h, :], mv[:, 0, h * T:(h + 1) * T],
                                                start=False, stop=True)
            last.then_inc(S("gla_o"), 1)
            pe.wait_ge(S("sgw_masked"), 1)
            pe.wait_ge(S("sv_done"), 2)
            pe.wait_ge(S("o_out"), 8)
            for tt in range(TT):
                for g in range(8):
                    last = nc.tensor.matmul(bank[4 + 2 * tt + g // 4][:, (g % 4) * P:(g % 4 + 1) * P], sgw[:, g, :],
                                            msv[:, tt, g * P:(g + 1) * P], start=True, stop=True)
                    if g % 4 == 3:
                        last.then_inc(S("sgu_mm"), 1)
            transposes("merged_T", "merged", go)
            pe.wait_ge(S("turned_lo"), turn("merged", 4, 4))
            m_group(T_WOUT2, "wout2")

            transposes("wq_T", "wq", xn)
            pe.wait_ge(S("turned_lo"), turn("wq", 4, 4))
            for n in range(2):
                f_tile((T_WQ + n) % R, T_WQ + n + 1, bank[4 + n][:, 0:T])
            for n in range(2, R):
                pe.wait_ge(S("pq_out"), n - 1)
                f_tile((T_WQ + n) % R, T_WQ + n + 1, bank[4 + n % 2][:, 0:T])
            with pe.Fori(0, N_WQ // R - 1) as i:
                for u in range(R):
                    pe.wait_ge(S("pq_out"), i * R + (R + u - 1))
                    f_tile(u, i * R + (T_WQ + R + u + 1), bank[4 + u % 2][:, 0:T])
            pe.wait_ge(S("keys_in"), 16)
            pe.wait_ge(S("pq_out"), 16)
            for q in range(8):
                if q >= 4:
                    pe.wait_ge(S("sc_out"), q - 3)
                for j in range(4):
                    n = 4 * q + j
                    tt, m = n // 16, n % 16
                    last = nc.tensor.matmul(bank[q % 4][:, j * P:(j + 1) * P], pq[:, m, tt * P:(tt + 1) * P],
                                            ky[:, m % 2, :], start=True, stop=True)
                last.then_inc(S("sc_mm"), 1)
            pe.wait_ge(S("chosen"), 1)
            for j, src in enumerate((t1f, t2f, tg)):
                for tt in range(TT):
                    last = nc.tensor.transpose(bank[4 + j // 2][:, (j % 2) * T + tt * P:(j % 2) * T + (tt + 1) * P],
                                               src[:, 8 * tt:8 * tt + 8, :], ident[:, :])
            last.then_inc(S("chosen_T"), 1)
            def weights4(b, count, copied):
                if copied is not None:
                    pe.wait_ge(S(f"g_copied{b}"), copied)
                for j in range(4):
                    pe.wait_ge(S("onehot"), count + (j + 1))
                    nc.tensor.matmul(bank[b][:, j * P:(j + 1) * P], oneB[:, j, :], oneA[:, j, :],
                                     start=True, stop=True).then_inc(S("onehot_used"), 1)

            for b in range(2):
                weights4(b, 4 * b, None)
            with pe.Fori(0, T // 8 - 1) as i:
                for b in range(2):
                    weights4(b, i * 8 + (8 + 4 * b), i + 1)
            pe.wait_ge(S("g_copied1"), T // 8)
            pairs(T_PEER, N_PEER, "peer", "peer")

        @block.vector
        def _(v):
            own = Steps(v, S("dve_steps"))
            tst, tsc, ttt, stt = nc.vector.tensor_tensor, nc.vector.tensor_scalar, nc.vector.tensor_tensor, \
                nc.vector.scalar_tensor_tensor

            def rs(name, tt):
                a = 2 * (RS_AT + SS[name]) + tt
                return st[:, a:a + 1]

            def scaled(name, key):
                v.wait_ge(S("roots"), rooted(name))
                for tt in range(TT):
                    tsc(xn[:, tt, :], xres[:, tt, :], rs(key, tt), None, ALU.mult).then_inc(S("unturned"), 1)

            def turned(group, name, gains, shifts=None):
                for b in range(4):
                    v.wait_ge(acc_ready, acc_filled(group, b))
                    for j in range(2):
                        k = 2 * b + j
                        src = bank[b][:, j * T:(j + 1) * T]
                        if gains is None:
                            ins = nc.vector.tensor_copy(xg[:, k, :], src)
                        elif shifts is None:
                            ins = tsc(xg[:, k, :], src, gains[:, k:k + 1], None, ALU.mult)
                        else:
                            ins = tsc(xg[:, k, :], src, gains[:, k:k + 1], shifts[:, k:k + 1], ALU.mult, ALU.add)
                        if j:
                            ins.then_inc(S("turned_xg"), 1)
                for b in range(4):
                    v.wait_ge(S("turned_hi"), turn(name, 4, b + 1))
                    last = ttt(xl[:, 2 * b:2 * b + 2, :], xg[:, 2 * b:2 * b + 2, :],
                               xh[:, 2 * b:2 * b + 2, :].bitcast(F32), ALU.subtract)
                    last.then_inc(S("turned_lo"), 1)

            def filled(group, b, tiles_end):
                if b < 3:
                    v.wait_ge(acc_ready, acc_filled(group, b))
                else:
                    v.wait_ge(tile_used, tiles_end)

            v.wait_ge(S("col_in"), 16)
            stt(tiny[:, 0:2], c_("lam"), -1.0, c_("lam"), ALU.mult, ALU.max).then_inc(S("lam_abs"), 1)
            scaled("mix", "mix")
            v.wait_ge(S("lam_exp"), 1)
            z, s, s2, acc, m = (tiny[:, 2 * j:2 * j + 2] for j in range(5))
            own(tsc(s2, z, 2.0, None, ALU.add)); own.sync()
            own(nc.vector.reciprocal(s2, s2)); own.sync()
            own(ttt(s, z, s2, ALU.mult)); own.sync()
            own(ttt(s2, s, s, ALU.mult)); own.sync()
            own(nc.vector.memset(acc, 1.0 / 17)); own.sync()
            for n in (15, 13, 11, 9, 7, 5, 3, 1):
                own(ttt(acc, acc, s2, ALU.mult)); own.sync()
                own(tsc(acc, acc, 1.0 / n, None, ALU.add)); own.sync()
            own(ttt(acc, acc, s, ALU.mult))
            own(tsc(m, c_("lam"), -1.0, 0.0, ALU.mult, ALU.max)); own.sync()
            own(stt(acc, acc, 2.0, m, ALU.mult, ALU.add)); own.sync()
            own(tsc(c8, acc, -8.0, None, ALU.mult))
            v.wait_ge(S("sil_sig"), 1)
            ttt(sil, sil, c_("c"), ALU.mult).then_inc(S("sil_done"), 1)
            turned("mix_T", "mix", c_("mix"))

            def chunks(a, n, dst, j0, done, scale=None):
                with v.Fori(0, n // 2) as i:
                    for u in range(2):
                        v.wait_ge(tile_used, i * 2 + (a + u + 1))
                        d_ = dst[:, bass.ds(i * 2 + (j0 + u), 1), :]
                        src = bank[4 + u][:, 0:T].unsqueeze(1)
                        if scale is None:
                            nc.vector.tensor_copy(d_, src).then_inc(done, 1)
                        else:
                            tsc(d_, src, scale, None, ALU.mult).then_inc(done, 1)

            chunks(T_IN_F, 8, zF, 0, S("in_f"))
            chunks(T_IN_F + 8, 4, zF, 8, S("in_f"), 0.125)
            chunks(T_IN_F + 12, 4, zF, 12, S("in_f"))
            for b in range(4):
                filled("in_M", b, T_WOUT)
                nc.vector.tensor_copy(zM[:, b // 2, (b % 2) * 512:(b % 2 + 1) * 512], bank[b][:, :])\
                    .then_inc(S("in_m"), 1)
            v.wait_ge(S("in_f"), 16)

            for c in range(2):
                own(tsc(xc[:, c, :], zF[:, c, :], c_("convw", 4 * c + 3), c_("convb", c), ALU.mult, ALU.add))
            for j in (2, 1, 0):
                own.sync()
                for c in range(2):
                    last = stt(xc[:, c, 3 - j:T], zF[:, c, 0:T - 3 + j], c_("convw", 4 * c + j),
                               xc[:, c, 3 - j:T], ALU.mult, ALU.add)
                    if j:
                        own(last)
            last.then_inc(S("xc_done"), 1)
            own(ttt(gy, zF[:, 2:4, :], zF[:, 2:4, :], ALU.mult)); own.sync()
            own(tsc(gy, gy, 0.044715, 1.0, ALU.mult, ALU.add)); own.sync()
            ttt(gy, gy, zF[:, 2:4, :], ALU.mult).then_inc(S("gy_arg"), 1)
            f_ = zF[:, 6:8, :]
            stt(h1, f_, -1.0, f_, ALU.mult, ALU.max).then_inc(S("hf_abs"), 1)
            v.wait_ge(S("hq_sig"), 1)
            own(ttt(hq, hq, zF[:, 4:6, :], ALU.mult))
            v.wait_ge(S("sg_sig"), 1)
            own(ttt(sg, sg, zM[:, :, 256:512], ALU.mult))
            v.wait_ge(S("gy_sig"), 1)
            own(ttt(gy, zF[:, 2:4, :], ld, ALU.mult))
            v.wait_ge(S("hf_ln"), 1)
            own(stt(h1, f_, 0.0, h1, ALU.min, ALU.subtract)); own.sync()
            own(tsc(hb, h1, LOG_TINY, None, ALU.subtract)); own.sync()
            stt(h2, hb, -1.0, hb, ALU.mult, ALU.max).then_inc(S("hf_abs"), 1)
            v.wait_ge(S("hf_ln"), 2)
            own(stt(h1, h1, LOG_TINY, h2, ALU.max, ALU.add)); own.sync()
            v.wait_ge(S("ones_set"), 1)
            for c in range(2):
                for tt in range(TT):
                    ts = slice(tt * P, (tt + 1) * P)
                    own(nc.vector.tensor_tensor_scan(hb[:, c, ts], ones, h1[:, c, ts], 0.0, ALU.mult, ALU.add))
            own(nc.vector.memset(hQ[:, :, :].rearrange("p a b -> p (a b)"), 0.0))
            v.wait_ge(S("hk_done"), 1)
            nc.vector.memset(hK[:, :, :].rearrange("p a b -> p (a b)"), 0.0).then_inc(S("h_qk"), 1)
            v.wait_ge(S("h_qk"), 1)
            own.sync()
            v.wait_ge(S("consts1_in"), 64)
            kf, qf, bf = (t_.rearrange("p a b -> p (a b)") for t_ in (hk, hq, hb))

            def level_diff(l):
                h = LEVELS[l]
                if l >= 2:
                    v.wait_ge(S("h_qk"), l)
                g_ = bf.rearrange("p (a n) -> p a n", n=2 * h)
                ttt(hdec[:, l % 2, :].rearrange("p (a n) -> p a n", n=2 * h), g_,
                    g_[:, :, h - 1:h].to_broadcast([P, 256 // h, 2 * h]), ALU.subtract).then_inc(S("h_diff"), 1)

            def level_qk(l):
                h = LEVELS[l]
                v.wait_ge(S("h_dec"), l + 1)
                if l >= 2:
                    v.wait_ge(S("h_sc"), 2 * l)
                sh = "p (a two h) -> p a two h"
                d_, k_, q_, K_, Q_ = (t_.rearrange(sh, two=2, h=h) for t_ in
                                      (hdec[:, l % 2, :], kf, qf, hK[:, l % 2, :], hQ[:, l % 2, :]))
                ttt(K_[:, :, 0, :], k_[:, :, 0, :], d_[:, :, 0, :], ALU.mult)
                ttt(Q_[:, :, 1, :], q_[:, :, 1, :], d_[:, :, 1, :], ALU.mult).then_inc(S("h_qk"), 1)

            def level_acc(l):
                for odd in range(2):
                    v.wait_ge(S("h_sc"), 2 * l + odd + 1)
                    if l:
                        v.wait_ge(S("h_acc"), 2 * (l - 1) + odd + 1)
                    src = bank[4 + 2 * (l % 2) + odd][:, :].rearrange("p (a b) -> p a b", a=4)
                    dst = att[:, 4 * odd:4 * odd + 4, :]
                    mk = msk[:, l:l + 1, :].bitcast(U32).to_broadcast([P, 4, P])
                    if l:
                        nc.vector.copy_predicated(dst, mk, src).then_inc(S("h_acc"), 1)
                    else:
                        ttt(dst, src, ident[:, :].unsqueeze(1).to_broadcast([P, 4, P]), ALU.mult)\
                            .then_inc(S("h_acc"), 1)

            level_diff(0)
            level_diff(1)
            for l in range(7):
                level_qk(l)
                if l + 2 < 7:
                    level_diff(l + 2)
                if l == 5:
                    v.wait_ge(S("h_qk"), 7)
                    ttt(hdec[:, 1, 0:256].rearrange("p (c t) -> p c t", c=2), hb[:, :, 0:P],
                        hb[:, :, P - 1:P].to_broadcast([P, 2, P]), ALU.subtract).then_inc(S("h_diff"), 1)
                level_acc(l)
            v.wait_ge(S("h_dec"), 8)
            x_ = hdec[:, 1, :].rearrange("p (s c t) -> p s c t", s=2, c=2)
            ttt(x_[:, 0], x_[:, 0], hk[:, :, 0:P], ALU.mult)
            ttt(x_[:, 1], x_[:, 1], hq[:, :, P:T], ALU.mult).then_inc(S("h_qk"), 1)
            level_acc(7)
            for odd in range(2):
                v.wait_ge(S("h_sc"), 17 + odd)
                nc.vector.tensor_copy(attx[:, 2 * odd:2 * odd + 2, :],
                                      bank[4 + odd][:, 0:T].rearrange("p (a b) -> p a b", a=2))\
                    .then_inc(S("h_acc"), 1)
            v.wait_ge(S("ri_done"), 1)
            for c in range(2):
                last = tsc(la[:, c, :], ri[:, c, :], c8[:, c:c + 1], None, ALU.mult)
            last.then_inc(S("la_done"), 1)
            v.wait_ge(S("h_o"), 1)
            o_ = bank[6][:, :].rearrange("p (a b) -> p a b", a=2)
            own(nc.vector.tensor_copy(y[:, :, 256:512], o_)); own.sync()
            own(ttt(h1, y[:, :, 256:512], y[:, :, 256:512], ALU.mult)); own.sync()
            nc.vector.tensor_reduce(hss, h1.rearrange("p a (h e) -> p (a h) e", h=4), AX.X, ALU.add)\
                .then_inc(S("hg_ss"), 1)
            v.wait_ge(S("a_done"), 1)
            own(ttt(la, lb_, lb_, ALU.mult)); own.sync()
            own(ttt(ld, ri[:, 2:4, :], xc, ALU.mult))
            stt(lc, la, 1.0, lc, ALU.add, ALU.mult).then_inc(S("lru_m2"), 1)
            v.wait_ge(S("roots"), rooted("hg"))
            for tt in range(TT):
                yv = y[:, tt, 256:512].rearrange("p (h e) -> p h e", h=4)
                own(ttt(yv, yv, hrs[:, 4 * tt:4 * tt + 4].unsqueeze(2).to_broadcast([P, 4, 64]), ALU.mult))
            own.sync()
            ttt(y[:, :, 256:512], y[:, :, 256:512], sg, ALU.mult).then_inc(S("hg_y"), 1)

            v.wait_ge(S("consts1_in"), 64)

            def a_soft(h):
                v.wait_ge(S("a_sc"), h + 1)
                if h >= 2:
                    v.wait_ge(S("a_exp"), h - 1)
                own(stt(sc[:, h % 2, :], ali, 2.0 ** -(h + 1), bank[6 + h % 2][:, 0:384], ALU.mult, ALU.add))
                own.sync()
                for tt, (a, b) in enumerate(((0, 128), (128, 384))):
                    own(nc.vector.tensor_reduce(nmx[:, 2 * h + tt:2 * h + tt + 1], sc[:, h % 2, a:b], AX.X, ALU.max))
                own.sync()
                tsc(nmx[:, 2 * h:2 * h + 2], nmx[:, 2 * h:2 * h + 2], -1.0, None, ALU.mult).then_inc(S("a_max"), 1)

            a_soft(0)
            for h in range(8):
                if h + 1 < 8:
                    a_soft(h + 1)
                v.wait_ge(S("a_tr"), h + 1)
                if h >= 2:
                    v.wait_ge(S("a_o"), h - 1)
                nc.vector.tensor_copy(pT[:, h % 2, :], bank[4 + h % 2][:, 0:384]).then_inc(S("a_pT"), 1)
            v.wait_ge(S("lru_sqrt"), 1)
            own(ttt(ld, ld, lc, ALU.mult)); own.sync()
            for c in range(2):
                own(nc.vector.tensor_tensor_scan(la[:, c, :], lb_[:, c, :], ld[:, c, :], 0.0, ALU.mult, ALU.add))
            own.sync()
            ttt(xc, la, gy, ALU.mult).then_inc(S("lru_h"), 1)
            v.wait_ge(S("lru_tr"), 1)
            nc.vector.tensor_copy(y[:, :, 0:256], bank[6][:, :].rearrange("p (a b) -> p a b", a=2))\
                .then_inc(S("lru_y"), 1)
            own(nc.vector.reciprocal(prs, psm))
            v.wait_ge(S("a_o"), 8)
            own.sync()
            for tt in range(TT):
                ttt(y[:, tt, 512:1024].rearrange("p (h e) -> p h e", h=8),
                    bank[tt][:, :].rearrange("p (h e) -> p h e", h=8),
                    prs.rearrange("p (h t) -> p h t", t=2)[:, :, tt:tt + 1].to_broadcast([P, 8, 64]),
                    ALU.mult).then_inc(S("att_y"), 1)
            v.wait_ge(ada_used, N_ADA)
            ttt(mod[:, :], bank[3][:, 0:48], c_("bada"), ALU.add).then_inc(S("mod_done"), 1)
            v.wait_ge(S("roots"), rooted("lru"))
            v.wait_ge(S("roots"), rooted("att"))
            for tt in range(TT):
                own(tsc(y[:, tt, 0:256], y[:, tt, 0:256], rs("lru", tt), None, ALU.mult))
            for tt in range(TT):
                tsc(y[:, tt, 512:1024], y[:, tt, 512:1024], rs("att", tt), None, ALU.mult).then_inc(S("unturned"), 1)
            turned("y_T", "y", c_("ygain"))

            def add_to_x(group, tiles_end, done):
                for b in range(4):
                    filled(group, b, tiles_end)
                    xv = xres[:, b // 2, (b % 2) * 512:(b % 2 + 1) * 512]
                    ttt(xv, xv, bank[b][:, :], ALU.add).then_inc(S(done), 1)

            add_to_x("wout", T_FFN, "x1_done")
            scaled("mlp", "mlp")
            turned("mlp_T", "mlp", c_("mlp"))

            def split_units(slot, name, n, used):
                v.wait_ge(S(name + "_gated"), n)
                if used is not None:
                    v.wait_ge(tile_used, used)
                nc.vector.tensor_copy(uh[:, slot, :], ua[:, slot, :]).then_inc(S(name + "_uh"), 1)
                v.wait_ge(S(name + "_uh"), n)
                ttt(ul[:, slot, :], ua[:, slot, :], uh[:, slot, :].bitcast(F32), ALU.subtract)\
                    .then_inc(S(name + "_lo"), 1)

            def hidden(base, count, name, gate):
                for i in range(2):
                    v.wait_ge(S(name + "_act"), i + 1)
                    gate(i, i).then_inc(S(name + "_gated"), 1)
                    split_units(i, name, i + 1, None)
                with v.Fori(0, (count - 2) // 2) as j:
                    for u in range(2):
                        v.wait_ge(S(name + "_act"), j * 2 + (3 + u))
                        gate(u, j * 2 + (2 + u)).then_inc(S(name + "_gated"), 1)
                        split_units(u, name, j * 2 + (3 + u), j * 4 + (base + 3 + 2 * u))

            hidden(T_FFN, N_FFN, "ffn", lambda s_, i: ttt(ua[:, s_, :], ua[:, s_, :], ua[:, s_, :], ALU.mult))
            add_to_x("ffn", T_IN2_F, "x2_done")
            v.wait_ge(S("roots"), rooted("fin"))
            v.wait_ge(S("consts1_in"), 64)
            for tt in range(TT):
                stt(xres[:, tt, :], xres[:, tt, :], rs("fin", tt), tmp, ALU.mult, ALU.mult).then_inc(S("fin_done"), 1)

            own(stt(gain[:, 0:8], mod[:, 8:16], 1.0, c_("n1"), ALU.add, ALU.mult))
            own(stt(gain[:, 8:16], mod[:, 32:40], 1.0, c_("n2"), ALU.add, ALU.mult))
            own.sync()
            v.wait_ge(S("fin_done"), 2)
            scaled("in2", "n1")
            turned("in2_T", "in2", gain[:, 0:8], mod[:, 0:8])
            with v.Fori(0, 2) as i:
                for u in range(2):
                    v.wait_ge(tile_used, i * 2 + (T_IN2_F + u + 1))
                    tsc(qk[:, bass.ds(i * 2 + u, 1), :], bank[4 + u][:, 0:T].unsqueeze(1), 128 ** -0.5, None,
                        ALU.mult).then_inc(S("qk_out"), 1)
            chunks(T_IN2_F + 4, 4, qk, 4, S("qk_out"))
            v.wait_ge(S("alr"), 1)
            nc.vector.tensor_copy(alT, bank[6][0:16, 0:T]).then_inc(S("alr_out"), 1)

            def read_out(group, tiles_end, dst, done):
                for b in range(4):
                    filled(group, b, tiles_end)
                    nc.vector.tensor_copy(dst[:, b // 2, (b % 2) * 512:(b % 2 + 1) * 512], bank[b][:, :])\
                        .then_inc(S(done), 1)

            read_out("m_v", T_IN2_M + 8, mv, "v_out")
            v.wait_ge(S("z_mm"), 1)
            for h in range(4):
                own(tsc(t2[:, h, :], bank[6 + h // 2][:, (h % 2) * T:(h % 2 + 1) * T], c_("balpha", h), None, ALU.add))
            own.sync()
            stt(t1, t2, -1.0, t2, ALU.mult, ALU.max).then_inc(S("z_abs"), 1)
            v.wait_ge(S("consts2_in"), 80)
            v.wait_ge(S("consts2_in"), 80)
            ttt(sgw, sgw, caus.unsqueeze(1).to_broadcast([P, 8, P]), ALU.mult).then_inc(S("sgw_masked"), 1)
            v.wait_ge(S("z_ln"), 1)
            own(stt(t2, t2, 0.0, t1, ALU.min, ALU.subtract)); own.sync()
            for h in range(4):
                for tt in range(TT):
                    ts = slice(tt * P, (tt + 1) * P)
                    own(nc.vector.tensor_tensor_scan(tG[:, h, ts], ones, t2[:, h, ts], 0.0, ALU.mult, ALU.add))
            own.sync()
            v8 = lambda t_: t_.rearrange("p a (b c) -> p (a b) c", b=2)
            ttt(v8(t1), v8(tG), v8(tG)[:, :, 63:64].to_broadcast([P, 8, P]), ALU.subtract).then_inc(S("g_diff"), 1)
            v.wait_ge(S("g_dec"), 1)
            ttt(t1[:, :, 0:P], tG[:, :, 0:P], tG[:, :, P - 1:P].to_broadcast([P, 4, P]), ALU.subtract)\
                .then_inc(S("g_diffx"), 1)
            ttt(t2, t2, qk[:, 0:4, :], ALU.mult)
            ttt(t3, t3, qk[:, 4:8, :], ALU.mult).then_inc(S("g_qk"), 1)
            v.wait_ge(S("g_dec"), 2)
            ttt(t1[:, :, 0:P], t1[:, :, 0:P], qk[:, 4:8, 0:P], ALU.mult)
            ttt(t1[:, :, P:T], t1[:, :, P:T], qk[:, 0:4, P:T], ALU.mult).then_inc(S("g_qk"), 1)
            read_out("m_r", T_IN2_M + 16, mr, "r_out")
            for g in range(2):
                for k in range(KC):
                    last = tsc(dg[:, k * P:(k + 1) * P], ident[:, :], mod[:, 16 + 24 * g + k:17 + 24 * g + k], None,
                               ALU.mult)
                last.then_inc(S("diag"), 1)
                for b in range(2):
                    v.wait_ge(S("gate_mm"), 2 * g + b + 1)
                    dst = (gate1 if g == 0 else gate2)[:, b * 512:(b + 1) * 512]
                    nc.vector.tensor_copy(dst, bank[4 + b][:, :]).then_inc(S("gates_done"), 1)
            v.wait_ge(S("r_sig"), 1)
            ttt(mr, mr, xn, ALU.mult).then_inc(S("r_gated"), 1)
            v.wait_ge(S("r_gated"), 1)
            v.wait_ge(S("consts2_in"), 80)
            own(ttt(mr, mr, rw[:, 0:1, :].to_broadcast([P, TT, D]), ALU.mult)); own.sync()
            for tt in range(TT):
                v.wait_ge(S("g_sc"), tt + 1)
                ttt(AT[:, 4 * tt:4 * tt + 4, :], bank[4 + tt][:, :].rearrange("p (a b) -> p a b", a=4),
                    caus.unsqueeze(1).to_broadcast([P, 4, P]), ALU.mult).then_inc(S("g_at"), 1)
            v.wait_ge(S("g_sc"), 3)
            nc.vector.tensor_copy(AT[:, 8:12, :], bank[6][:, :].rearrange("p (a b) -> p a b", a=4))\
                .then_inc(S("g_at"), 1)
            v.wait_ge(S("ga_out"), 4)
            own(ttt(mr, mr, mga, ALU.mult))
            v.wait_ge(S("sv_out"), 4)
            sums = st[:, 2 * SS["sgs"]:2 * SS["sgs"] + 4].rearrange("p (a b) -> p a b", a=2)
            own(ttt(s_(SS["sgm"]).unsqueeze(2), sums[:, :, 0:1], sums[:, :, 1:2], ALU.add)); own.sync()
            tsc(s_(SS["sgm"]), s_(SS["sgm"]), -1.0 / D, None, ALU.mult).then_inc(S("sg_mean"), 1)
            own(ttt(msu, msu, mgb, ALU.mult))
            v.wait_ge(S("roots"), rooted("sgv"))
            v.wait_ge(S("sg_mean"), 1)
            for tt in range(TT):
                own(tsc(msv[:, tt, :], msv[:, tt, :], s_(SS["sgm"])[:, tt:tt + 1], rs("sgv", tt), ALU.add, ALU.mult))
                own.sync()
                own(ttt(msv[:, tt, :], msv[:, tt, :], rw[:, 1, :], ALU.mult)); own.sync()
                ttt(msv[:, tt, :], msv[:, tt, :], rw[:, 2, :], ALU.add).then_inc(S("sv_done"), 1)
            v.wait_ge(S("roots"), rooted("gla"))
            for tt in range(TT):
                for h in range(4):
                    n = 4 * tt + h
                    stt(go[:, tt, h * T:(h + 1) * T], bank[4 + 2 * tt + h // 2][:, (h % 2) * T:(h % 2 + 1) * T],
                        grs[:, n:n + 1], mr[:, tt, h * T:(h + 1) * T], ALU.mult, ALU.mult).then_inc(S("o_out"), 1)
            for tt in range(TT):
                for g in range(8):
                    if g % 4 == 0:
                        v.wait_ge(S("sgu_mm"), 2 * tt + g // 4 + 1)
                    cs = slice(g * P, (g + 1) * P)
                    own(stt(msu[:, tt, cs], bank[4 + 2 * tt + g // 4][:, (g % 4) * P:(g % 4 + 1) * P], c_("sgb", g),
                            msu[:, tt, cs], ALU.add, ALU.mult))
                own.sync()
                ttt(go[:, tt, :], go[:, tt, :], msu[:, tt, :], ALU.add).then_inc(S("unturned"), 1)
            turned("merged_T", "merged", None)
            for b in range(4):
                filled("wout2", b, T_WQ)
                own(ttt(msv[:, b // 2, (b % 2) * 512:(b % 2 + 1) * 512], bank[b][:, :],
                        gate1[:, (b % 2) * 512:(b % 2 + 1) * 512], ALU.mult))
                own.sync()
                xv = xres[:, b // 2, (b % 2) * 512:(b % 2 + 1) * 512]
                ttt(xv, xv, msv[:, b // 2, (b % 2) * 512:(b % 2 + 1) * 512], ALU.add).then_inc(S("x3_done"), 1)
            scaled("wq", "n2")
            turned("wq_T", "wq", gain[:, 8:16], mod[:, 24:32])
            chunks(T_WQ, 16, pq, 0, S("pq_out"))

            for q in range(8):
                v.wait_ge(S("sc_mm"), q + 1)
                nc.vector.tensor_copy(scs[:, 4 * q:4 * q + 4, :], bank[q % 4][:, :].rearrange("p (a b) -> p a b", a=4))\
                    .then_inc(S("sc_out"), 1)
            LOWEST = -3.0e38

            def best16(vals, work, top_v, top_i, lists):
                for n in lists:
                    own(nc.vector.max(top_v[:, n, 0:8], vals[:, n, :]))
                own.sync()
                for n in lists:
                    own(nc.vector.max_index(top_i[:, n, 0:8].bitcast(U32), top_v[:, n, 0:8], vals[:, n, :]))
                    own(nc.vector.match_replace(work[:, n, :], top_v[:, n, 0:8], vals[:, n, :], LOWEST))
                own.sync()
                for n in lists:
                    own(nc.vector.max(top_v[:, n, 8:16], work[:, n, :]))
                own.sync()
                for n in lists:
                    own(nc.vector.max_index(top_i[:, n, 8:16].bitcast(U32), top_v[:, n, 8:16], work[:, n, :]))
                own.sync()

            v.wait_ge(S("sc_out"), 8)
            best16(scs, scr, pv, pI, range(32))
            own(nc.vector.tensor_copy(pIf, pI.bitcast(U32))); own.sync()
            v1, v2 = (pv.rearrange("p (l s) n -> p l s n", s=2)[:, :, s_2, :] for s_2 in range(2))
            i1, i2 = (pIf.rearrange("p (l s) n -> p l s n", s=2)[:, :, s_2, :] for s_2 in range(2))
            own(tsc(i1, i1, 128.0, None, ALU.mult)); own.sync()
            for a1, a2, dst in ((v1, v2, cand), (i1, i2, cidx)):
                for a in range(8):
                    n = 16 // (a + 1)
                    at = PAIRS.index((a, 0))
                    own(ttt(dst[:, :, at:at + n], a1[:, :, a:a + 1].to_broadcast([P, 16, n]), a2[:, :, 0:n], ALU.add))
                at = PAIRS.index((8, 0))
                own(ttt(dst[:, :, at:at + 8], a1[:, :, 8:16], a2[:, :, 0:1].to_broadcast([P, 16, 8]), ALU.add))
            own.sync()
            best16(cand, cand2, tv, tp, range(16))
            own(nc.vector.tensor_copy(tpf, tp.bitcast(U32)))
            ttt(tg, tv, tv[:, :, 0:1].to_broadcast([P, 16, 16]), ALU.subtract).then_inc(S("top_shift"), 1)
            own.sync()
            v.wait_ge(S("iota_in"), 16)
            for tt in range(TT):
                ls = slice(8 * tt, 8 * tt + 8)
                e4 = eqs.rearrange("p (l k) n -> p l k n", l=8)
                for l in range(8):
                    own(ttt(e4[:, l], tpf[:, 8 * tt + l, :].unsqueeze(2).to_broadcast([P, 16, NPAIR]),
                            iot[:, 0:NPAIR].unsqueeze(1).to_broadcast([P, 16, NPAIR]), ALU.is_equal))
                own.sync()
                for l in range(8):
                    own(ttt(e4[:, l], e4[:, l], cidx[:, 8 * tt + l, :].unsqueeze(1).to_broadcast([P, 16, NPAIR]),
                            ALU.mult))
                own.sync()
                own(nc.vector.tensor_reduce(tid[:, ls, :].rearrange("p a b -> p (a b)"), eqs, AX.X, ALU.add))
                own.sync()
            own(nc.vector.tensor_copy(tiu.bitcast(U32), tid)); own.sync()
            own(tsc(tp.bitcast(U32), tiu.bitcast(U32), 7, None, ALU.logical_shift_right))
            own(tsc(tiu.bitcast(U32), tiu.bitcast(U32), 127, None, ALU.bitwise_and)); own.sync()
            own(nc.vector.tensor_copy(t1f, tp.bitcast(U32)))
            own(nc.vector.tensor_copy(t2f, tiu.bitcast(U32)))
            v.wait_ge(S("top_exp"), 1)
            own(nc.vector.tensor_reduce(tsm, tg, AX.X, ALU.add)); own.sync()
            own(nc.vector.reciprocal(trs, tsm)); own.sync()
            ttt(tg, tg, trs.unsqueeze(2).to_broadcast([P, 16, 16]), ALU.mult).then_inc(S("chosen"), 1)
            v.wait_ge(S("chosen_T"), 1)
            own(nc.vector.tensor_copy(i1T, bank[4][:, 0:T]))
            own(nc.vector.tensor_copy(i2T, bank[4][:, T:2 * T]))
            own(nc.vector.tensor_copy(gT, bank[5][:, 0:T]))
            own.sync()
            def onehots(t, j, used):
                if used is not None:
                    v.wait_ge(S("onehot_used"), used)
                nc.vector.tensor_scalar(oneB[:, j, :], iot, i2T[:, bass.ds(t, 1)], None, ALU.is_equal)
                nc.vector.tensor_scalar(oneA[:, j, :], iot, i1T[:, bass.ds(t, 1)], gT[:, bass.ds(t, 1)],
                                        ALU.is_equal, ALU.mult).then_inc(S("onehot"), 1)

            for j in range(4):
                onehots(j, j, None)
            with v.Fori(0, T // 4 - 1) as i:
                for j in range(4):
                    onehots(i * 4 + (4 + j), j, i * 4 + (j + 1))
            hidden(T_PEER, N_PEER, "peer",
                   lambda s_, i: ttt(ua[:, s_:s_ + 1, :].rearrange("p a t -> p t a"),
                                     ua[:, s_:s_ + 1, :].rearrange("p a t -> p t a"), G[:, :, bass.ds(i, 1)], ALU.mult))
            v.wait_ge(S("last_in"), 48)
            v.wait_ge(S("last_in"), 48)
            for b in range(4):
                filled("peer", b, T_END)
                cs = slice((b % 2) * 512, (b % 2 + 1) * 512)
                own(ttt(fin_t[:, b // 2, cs], bank[b][:, :], fin_g[:, cs], ALU.mult)); own.sync()
                ttt(fin_x[:, b // 2, cs], fin_x[:, b // 2, cs], fin_t[:, b // 2, cs], ALU.add)\
                    .then_inc(S("x4_done"), 1)
            v.wait_ge(S("roots"), rooted("last"))
            v.wait_ge(S("last_in"), 48)
            for tt in range(TT):
                stt(fin_o[:, tt, :], fin_x[:, tt, :], rs("last", tt), fin_w, ALU.mult, ALU.mult)\
                    .then_inc(S("out_done"), 1)


def f_tiles(w):
    n = w.shape[1] // P
    return w.reshape(KC, P, n, P).transpose(2, 1, 0, 3).reshape(n, P, D)


def columns(v_):
    return v_.reshape(-1, P).T


def interleave(f, m):
    order = [f[0]]
    for i in range(len(f) - 1):
        order += [f[i + 1], m[i]]
    return order + [m[len(m) - 1]]


def kernel(**inputs):
    import concourse.bacc as bacc
    from concourse.bass_utils import run_bass_kernel_spmd

    a = {k: np.asarray(v_) for k, v_ in inputs.items()}
    w_in, w_in2 = a["w_in"][0], a["w_in_2"][0]
    at = np.cumsum([0, 512, 512, 1024, 1024, 16, 1024, 1024, 1024, 1024])
    q2, k2, v2, r2, alr, su, sv, ga, gb = (w_in2[:, at[j]:at[j + 1]] for j in range(9))
    tiles = list(f_tiles(np.concatenate([w_in[:, 0:1024], w_in[:, 1536:2560]], 1)))
    tiles += list(np.concatenate([w_in[:, 1024:1536], w_in[:, 2560:3072]], 1).reshape(KC, P, D))
    tiles += list(a["w_out"][0].reshape(KC, P, D))
    tiles += interleave(f_tiles(a["w_ff1"][0]), a["w_ff2"][0].reshape(N_FFN, P, D))
    tiles += list(f_tiles(np.concatenate([q2, k2], 1)))
    for w in (v2, r2, ga, gb, su, sv):
        tiles += list(w.reshape(KC, P, D))
    tiles += list(a["w_out_2"][0].reshape(KC, P, D))
    tiles += list(f_tiles(a["peer_w_q_2"][0]))
    down = a["peer_down_2"][0].reshape(N_PEER, P, KC, P).transpose(0, 3, 2, 1).reshape(N_PEER, P, D)
    tiles += interleave(down, a["peer_up_2"][0].reshape(N_PEER, P, D))
    hg = a["hg_norm_w"][0]
    cols = np.concatenate([
        columns(a["norm_mix"][0]), columns(a["norm_mlp"][0]), columns(a["norm1_w_2"][0]), columns(a["norm2_w_2"][0]),
        columns(np.concatenate([a["lru_out_norm"][0], hg, hg, hg, hg, a["att_out_norm"][0]])),
        columns(a["b_ada_2"][0]), columns(a["c_2"][0]),
        a["lru_conv_w"][0].reshape(4, 2, P).transpose(2, 1, 0).reshape(P, 8), columns(a["lru_conv_b"][0]),
        columns(a["lru_ba"][0]), columns(a["lru_bx"][0]), columns(a["lru_lambda"][0]), columns(a["b_alpha_2"][0]),
        a["sgu_b_2"][0].T], 1)
    rows = np.concatenate([a["norm_final"], a["gla_norm_w_2"][0], a["sgu_ln_w_2"][0], a["sgu_ln_b_2"][0],
                           a["final_norm_w_2"]])[None]
    lru = [a[n][0].reshape(2, 2, 64, 64).transpose(1, 2, 0, 3).reshape(P, 128) for n in ("lru_wa", "lru_wx")]
    s, t = np.arange(P)[:, None], np.arange(P)[None, :]
    masks = [np.zeros((P, P), bool)]
    for h in LEVELS:
        masks.append((s // (2 * h) == t // (2 * h)) & (s % (2 * h) < h) & (t % (2 * h) >= h))
    rel = [np.where(k - q <= 0, k - q, -2.56e32) for q, k in
           ((np.arange(P)[:, None], np.arange(P)[None, :]), (P + np.arange(P)[:, None], np.arange(T)[None, :]))]
    arrays = {
        "x": a["x"][0].reshape(TT, P, D).transpose(1, 0, 2).reshape(P, TT * D),
        "stream": np.stack(tiles).reshape(T_END * P, D),
        "ada": f_tiles(a["w_ada_2"][0]).reshape(N_ADA * P, D),
        "cols": cols, "rows": rows, "lru_w": np.concatenate(lru, 1),
        "hgmask": np.concatenate(masks, 1).astype(np.uint32),
        "causal": (s <= t).astype(np.float32),
        "alibi": np.concatenate(rel, 1).astype(np.float32),
        "iota": np.concatenate([np.broadcast_to(t, (P, P)), np.eye(P)], 1).astype(np.float32),
        "walr": alr.reshape(KC, P, 16).transpose(1, 0, 2).reshape(P, P),
        "wup": a["w_alpha_up_2"][0],
        "sguw": a["sgu_w_2"][0].transpose(2, 0, 1).reshape(P, D),
        "keys": np.concatenate([a["peer_keys1_2"][0].T, a["peer_keys2_2"][0].T], 1),
    }
    nc = bacc.Bacc("TRN2", target_bir_lowering=False, num_devices=1)
    args = {}
    for name, v_ in arrays.items():
        arrays[name] = v_ = np.ascontiguousarray(v_)
        args[name] = nc.dram_tensor(name, v_.shape, mybir.dt.from_np(v_.dtype), kind="ExternalInput").ap()
    args["out"] = nc.dram_tensor("out", (T, D), F32, kind="ExternalOutput").ap()
    build(nc, **args)
    r = run_bass_kernel_spmd(nc, [arrays], core_ids=[0])
    return r.results[0]["out"].reshape(1, T, D)
```

```python
import concourse.bass as bass
from concourse import mybir
from concourse.alu_op_type import AluOpType as ALU
from contextlib import ExitStack
import numpy as np

F32 = mybir.dt.float32
F32R = mybir.dt.float32r
U32 = mybir.dt.uint32
BF16 = mybir.dt.bfloat16
ACT = mybir.ActivationFunctionType
AX = mybir.AxisListType

P = 128
D = 1024
T = 256
TT = T // P
KC = D // P
EPS = 1e-6
LOG_TINY = float(np.log(np.float32(1e-30)))
NEXP_ROWS = 128
R = 4

N_IN_F, N_IN_M, N_WOUT, N_FFN, N_IN2_F, N_IN2_M, N_WOUT2, N_WQ, N_PEER = 16, 8, 8, 32, 8, 48, 8, 16, NEXP_ROWS
T_IN_F = 0
T_IN_M = T_IN_F + N_IN_F
T_WOUT = T_IN_M + N_IN_M
T_FFN = T_WOUT + N_WOUT
T_IN2_F = T_FFN + 2 * N_FFN
T_IN2_M = T_IN2_F + N_IN2_F
T_WOUT2 = T_IN2_M + N_IN2_M
T_WQ = T_WOUT2 + N_WOUT2
T_PEER = T_WQ + N_WQ
T_UP = T_PEER + N_PEER
T_END = T_UP + N_PEER
HALF = N_PEER // 2
N_ADA = 48
ADA_FIRST = 32

GROUPS = ["mix_T", "in_M", "y_T", "wout", "mlp_T", "ffn", "in2_T", "m_sv", "m_su", "m_v", "m_r",
          "m_ga", "m_gb", "merged_T", "wout2", "wq_T", "peer"]
TRANSPOSES = ["mix_T", "y_T", "mlp_T", "in2_T", "merged_T", "wq_T"]
READ_OUT = {"in_M": "in_m", "wout": "x1_done", "ffn": "x2_done", "m_v": "v_out", "m_r": "r_out",
            "m_ga": "ga_out", "m_gb": "gb_out", "m_su": "su_out", "m_sv": "sv_out", "wout2": "x3_done"}


def acc_freed(group, bank):
    before = GROUPS[:GROUPS.index(group)]
    if not before or group == "peer":
        return None
    last = before[-1]
    return ("turned_xg", turn(last[:-2], 4, bank + 1)) if last in TRANSPOSES else (READ_OUT[last], bank + 1)


def acc_filled(group, bank):
    before = GROUPS[:GROUPS.index(group)]
    return sum(4 if g in TRANSPOSES else 3 for g in before) + bank + 1


COLS = {}
_at = 0
for _name, _n in [("mix", 8), ("mlp", 8), ("n1", 8), ("n2", 8), ("ygain", 8), ("bada", 32), ("c", 8),
                  ("convw", 8), ("convb", 2), ("ba", 2), ("bx", 2), ("lam", 2), ("balpha", 4), ("sgb", 8)]:
    COLS[_name] = (_at, _at + _n)
    _at += _n
NCOLS = _at

LEVELS = [1, 2, 4, 8, 16, 32, 64]
PAIRS = [(a, b) for a in range(16) for b in range(16) if (a + 1) * (b + 1) <= 16]
NPAIR = len(PAIRS)


TURNS = ["mix", "y", "mlp", "in2", "merged", "wq"]
SQUARES = ["mix", "lru", "att", "mlp", "fin", "in2", "sgv", "wq", "last"]
ROOTS = ["mix", "lru", "att", "hg", "mlp", "fin", "in2", "sgv", "gla", "wq", "last"]


def turn(name, per, n):
    return per * TURNS.index(name) + n


def squared(name, n=2):
    return 2 * SQUARES.index(name) + n


def rooted(name):
    return ROOTS.index(name) + 1


class Steps:

    def __init__(self, eng, sem):
        self.eng, self.sem, self.n = eng, sem, 0

    def __call__(self, ins):
        ins.then_inc(self.sem, 1)
        self.n += 1
        return self.n

    def sync(self):
        self.eng.wait_ge(self.sem, self.n)


def build(nc, x, stream, ada, cols, rows, lru_w, hgmask, causal, alibi, iota, walr, wup, sguw, keys, out):
    ctx = ExitStack()
    with ctx:
        def sb(name, shape, dt=F32):
            return ctx.enter_context(nc.sbuf_tensor(name, shape, dt))

        sems = {}

        def S(name):
            if name not in sems:
                sems[name] = ctx.enter_context(nc.semaphore(name))
            return sems[name]

        raw = sb("raw", [P, R, 1024])
        whi = sb("whi", [P, R, 1024], F32R)
        wlo = sb("wlo", [P, R, 1024], F32R)
        xh = sb("xh", [P, KC, T], F32R)
        xl = sb("xl", [P, KC, T], F32R)
        ua = sb("ua", [P, 2, T])
        uh = sb("uh", [P, 2, T], F32R)
        ul = sb("ul", [P, 2, T], F32R)
        xs = sb("xs", [P, TT * D])
        ident = sb("ident", [P, P])
        col = sb("col", [P, NCOLS])
        st = sb("st", [P, 64])
        mod = sb("mod", [P, 32])
        arena = sb("arena", [P, 32768])
        xres = xs[:, :].rearrange("p (a d) -> p a d", a=TT)
        rest = xs[:, 640:896]
        picks = xs[:, 0:640].bitcast(BF16).rearrange("p (s t) -> p s t", s=5)
        same = xs[:, 640:896].rearrange("p (t n) -> p t n", t=4)
        oneA = xs[:, 896:1664].bitcast(BF16).rearrange("p (r s t n) -> p r s t n", r=2, s=3, t=4)
        iot = xs[:, 1664:1792]
        oneB = ua[:, :, :].rearrange("p a b -> p (a b)").bitcast(BF16).rearrange("p (r t n) -> p r t n", r=2, t=4)
        x_spill = nc.dram_tensor("x_spill", [P, TT * D], F32, kind="Internal").ap()
        g_spill = nc.dram_tensor("g_spill", [P, D], F32, kind="Internal").ap()

        top = [0]

        def take(n, *dims):
            a = arena[:, top[0]:top[0] + n]
            top[0] += n
            assert top[0] <= 32768, top[0]
            if len(dims) == 2:
                a = a.rearrange("p (a b) -> p a b", a=dims[0])
            if len(dims) == 3:
                a = a.rearrange("p (a b c) -> p a b c", a=dims[0], b=dims[1])
            return a

        xn = take(2048, TT, D)
        xg = take(2048, KC, T)
        tmp = take(1024)
        ones = take(128)
        neghalf, sil = st[:, 48:56], st[:, 56:64]
        gate1 = take(1024)
        gate2 = take(1024)
        shared = top[0]
        zF = take(4096, 16, T)
        zM = take(2048, TT, D)
        y = take(2048, TT, D)
        adar = take(4096, R, 1024)
        lw = take(256, 4, 64)
        c8 = take(2)
        tiny = take(16)
        xc, la, lb_, lc, ld, gy = (take(512, 2, T) for _ in range(6))
        ri = take(1024, 4, T)
        hk, hq, hb, h1, h2 = (take(512, 2, T) for _ in range(5))
        hdec = take(1024, 2, 512)
        hQ = take(1024, 2, 512)
        hK = take(1024, 2, 512)
        att = take(1024, 8, P)
        attx = take(512, 4, P)
        msk = take(1024, 8, P)
        ali = take(384)
        xg_, xn_ = (t_.rearrange("p a b -> p (a b)") for t_ in (xg, xn))
        sc, pp = (xg_[:, n:n + 768].rearrange("p (a b) -> p a b", a=2) for n in (0, 768))
        pT = xn_[:, 0:768].rearrange("p (a b) -> p a b", a=2)
        sg = xg_[:, 1536:2048].rearrange("p (a b) -> p a b", a=2)
        nmx, psm, prs = take(16), take(16), take(16)
        hss, hrs = take(8), take(8)
        top[0] = shared
        qk = take(2048, 8, T)
        mv, mr, mga, mgb, msu, msv = (take(2048, TT, D) for _ in range(6))
        t1, t2, t3, tG = (take(1024, 4, T) for _ in range(4))
        adar2 = arena[:, top[0] - 4096:top[0]].rearrange("p (r n) -> p r n", r=R)
        AT = take(1536, 12, P)
        go = take(2048, TT, D)
        rw = take(2048, 2, D)
        gla_w = tmp
        sgw = take(1024, 8, P)
        caus = take(128)
        wal = take(128, KC, 16)
        wupt = t1.rearrange("p a b -> p (a b)")[0:16, 0:512]
        alT = t1.rearrange("p a b -> p (a b)")[0:16, 512:768]
        gss, grs = take(8), take(8)
        gain = take(16)
        top[0] = shared
        pq = take(4096, 16, T)
        top[0] = 16384
        ky = take(256, 2, P)
        scs = take(4096, 32, P)
        scr = take(4096, 32, P)
        eqs = arena[:, 16640:16640 + 8 * 16 * NPAIR].rearrange("p (a b) -> p a b", b=NPAIR)
        pv = take(512, 32, 16)
        pI = take(512, 32, 16)
        pIf = take(512, 32, 16)
        cand = take(16 * NPAIR, 16, NPAIR)
        cidx = take(16 * NPAIR, 16, NPAIR)
        cand2 = take(16 * NPAIR, 16, NPAIR)
        tv = take(256, 16, 16)
        tp = take(256, 16, 16)
        tpf = take(256, 16, 16)
        tid = take(256, 16, 16)
        tiu = take(256, 16, 16)
        t1f = take(256, 16, 16)
        t2f = take(256, 16, 16)
        tg = take(256, 16, 16)
        tsm, trs = take(16), take(16)
        units3 = arena[:, :].rearrange("p (n t) -> p n t", t=T)
        fin_t = arena[:, 2048:4096].rearrange("p (a d) -> p a d", a=TT)
        fin_g = arena[:, 4096:5120]
        fin_w = arena[:, 5120:6144]
        fin_o = arena[:, 6144:8192].rearrange("p (a d) -> p a d", a=TT)

        bank = [ctx.enter_context(nc.psum_tensor(f"bank{i}", [P, 512], F32)) for i in range(8)]

        def c_(name, j=None, n=1):
            a, b = COLS[name]
            return col[:, a:b] if j is None else col[:, a + j:a + j + n]

        def s_(k, n=2):
            return st[:, 2 * k:2 * k + n]

        SS = dict(mix=0, lru=1, att=2, mlp=3, fin=4, n1=5, sgm=6, sgv=7, n2=8, last=9, sgs=10)
        RS_AT = 12

        raw_full = [S(f"raw_full{s}") for s in range(R)]
        ada_full = [S(f"ada_full{s}") for s in range(R)]
        hi_done, lo_done, tile_used = S("hi_done"), S("lo_done"), S("tile_used")
        acc_ready = S("acc_ready")
        ada_used = S("ada_used")

        block = ctx.enter_context(nc.Block())

        @block.sync
        def _(sp):
            def tile(slot, row, free):
                if free is not None:
                    sp.wait_ge(lo_done, free)
                sp.dma_start(raw[:, slot, :], stream[bass.ds(row, P), :]).then_inc(raw_full[slot], 16)

            for tt in range(TT):
                sp.dma_start(xres[:, tt, :], x[:, tt * D:(tt + 1) * D]).then_inc(S(f"x_in{tt}"), 16)
            sp.dma_start(col[:, :], cols).then_inc(S("col_in"), 16)
            sp.dma_start(ident[:, :], iota[:, P:2 * P]).then_inc(S("ident_in"), 16)
            for n in range(R):
                tile(n, n * P, None)
            sp.dma_start(lw.rearrange("p a b -> p (a b)"), lru_w).then_inc(S("consts1_in"), 16)
            sp.dma_start(msk.rearrange("p a b -> p (a b)").bitcast(U32), hgmask).then_inc(S("consts1_in"), 16)
            sp.dma_start(tmp, rows[:, 0:D].to_broadcast([P, D])).then_inc(S("consts1_in"), 16)
            sp.dma_start(ali, alibi).then_inc(S("consts1_in"), 16)
            sp.dma_start(gate1, rows[:, 5 * D:6 * D].to_broadcast([P, D])).then_inc(S("gate1_b"), 16)

            for n in range(R):
                sp.dma_start(adar[:, n, :], ada[n * P:(n + 1) * P, :]).then_inc(ada_full[n], 16)

            def ada_loads(a, b):
                with sp.Fori(0, (b - a) // R) as i:
                    for u in range(R):
                        sp.wait_ge(ada_used, i * R + (a - R + u + 1))
                        sp.dma_start(adar[:, u, :], ada[bass.ds(i * (R * P) + (a + u) * P, P), :])\
                            .then_inc(ada_full[u], 16)

            with sp.Fori(0, (T_WOUT + 4 - R) // R) as i:
                for u in range(R):
                    tile(u, i * (R * P) + (R + u) * P, i * R + (u + 1))
            ada_loads(R, 12)
            for n in range(T_WOUT + 4, T_WOUT + 8):
                tile(n % R, n * P, n - R + 1)
            ada_loads(12, 16)
            for n in range(T_FFN, T_FFN + 8):
                tile(n % R, n * P, n - R + 1)
            ada_loads(16, 24)
            with sp.Fori(0, (T_IN2_F - T_FFN) // R - 1) as i:
                for u in range(R):
                    tile(u, i * (R * P) + (T_FFN + 8 + u) * P, i * R + (T_FFN + 8 - R + u + 1))
            for n in range(T_IN2_F + 4, T_IN2_F + 7):
                tile(n % R, n * P, n - R + 1)
            ada_loads(24, 32)
            tile((T_IN2_F + 7) % R, (T_IN2_F + 7) * P, T_IN2_F + 7 - R + 1)
            sp.wait_ge(S("fin_done"), 2)
            sp.dma_start(wal.rearrange("p a b -> p (a b)"), walr).then_inc(S("consts2_in"), 16)
            sp.dma_start(wupt, wup).then_inc(S("consts2_in"), 16)
            sp.dma_start(rw.rearrange("p a b -> p (a b)"), rows[:, 2 * D:4 * D].to_broadcast([P, 2 * D]))\
                .then_inc(S("consts2_in"), 16)
            sp.dma_start(sgw.rearrange("p a b -> p (a b)"), sguw).then_inc(S("consts2_in"), 16)
            sp.dma_start(gla_w, rows[:, D:2 * D].to_broadcast([P, D])).then_inc(S("consts2_in"), 16)
            sp.dma_start(caus, causal).then_inc(S("consts2_in"), 16)
            with sp.Fori(0, (T_IN2_M + 40 - T_IN2_F - 8) // R) as i:
                for u in range(R):
                    tile(u, i * (R * P) + (T_IN2_F + 8 + u) * P, i * R + (T_IN2_F + 8 - R + u + 1))
            sp.wait_ge(S("mod_done"), 1)
            sp.dma_start(gate2, rows[:, 6 * D:7 * D].to_broadcast([P, D])).then_inc(S("gate2_b"), 16)
            sp.wait_ge(S("g_sc"), 3)

            def ada2_loads(a):
                for n in range(a, a + R):
                    if n >= ADA_FIRST + R:
                        sp.wait_ge(ada_used, n - R + 1)
                    sp.dma_start(adar2[:, n % R, :], ada[n * P:(n + 1) * P, :]).then_inc(ada_full[n % R], 16)

            ada2_loads(ADA_FIRST)
            for n in range(T_IN2_M + 40, T_WOUT2 + 7):
                tile(n % R, n * P, n - R + 1)
            ada2_loads(ADA_FIRST + 4)
            tile((T_WOUT2 + 7) % R, (T_WOUT2 + 7) * P, T_WOUT2 + 7 - R + 1)
            ada2_loads(ADA_FIRST + 8)
            for n in range(T_WQ, T_WQ + 7):
                tile(n % R, n * P, n - R + 1)
            ada2_loads(ADA_FIRST + 12)
            tile((T_WQ + 7) % R, (T_WQ + 7) * P, T_WQ + 7 - R + 1)
            sp.wait_ge(S("unturned"), turn("wq", 2, 2))
            sp.dma_start(x_spill, xs[:, :]).then_inc(S("spilled"), 16)
            sp.wait_ge(S("ada_out"), 12)
            sp.dma_start(g_spill, gate2).then_inc(S("spilled"), 16)
            sp.wait_ge(S("spilled"), 32)
            sp.dma_start(iot, iota[:, 0:P]).then_inc(S("iota_in"), 16)
            sp.wait_ge(S("turned_lo"), turn("wq", 4, 4))
            sp.dma_start(ky.rearrange("p a b -> p (a b)"), keys).then_inc(S("keys_in"), 16)
            with sp.Fori(0, (T_UP + HALF - T_WQ) // R) as i:
                for u in range(R):
                    tile(u, i * (R * P) + (T_WQ + 8 + u) * P, i * R + (T_WQ + 8 - R + u + 1))
            sp.wait_ge(S("weighted"), 2 + N_PEER)
            sp.dma_start(xs[:, :], x_spill).then_inc(S("last_in"), 16)
            sp.wait_ge(S("u_lo"), HALF)
            sp.dma_start(fin_g, g_spill).then_inc(S("last_in"), 16)
            sp.dma_start(fin_w, rows[:, 4 * D:5 * D].to_broadcast([P, D])).then_inc(S("last_in"), 16)
            with sp.Fori(0, (T_END - T_UP - HALF - 8) // R) as i:
                for u in range(R):
                    tile(u, i * (R * P) + (T_UP + HALF + 8 + u) * P, i * R + (T_UP + HALF + 8 - R + u + 1))
            for tt in range(TT):
                sp.wait_ge(S("out_done"), tt + 1)
                sp.dma_start(out[tt * P:(tt + 1) * P, :], fin_o[:, tt, :]).then_inc(S("stored"), 16)
            sp.wait_ge(S("stored"), 16 * TT)

        @block.gpsimd
        def _(pool):
            def lo(slot, count):
                pool.wait_ge(hi_done, count)
                nc.gpsimd.tensor_tensor(wlo[:, slot, :], raw[:, slot, :], whi[:, slot, :].bitcast(F32),
                                        ALU.subtract).then_inc(lo_done, 1)

            def los(a, b):
                with pool.Fori(0, (b - a) // R) as i:
                    for u in range(R):
                        lo((a + u) % R, i * R + (a + u + 1))

            own = Steps(pool, S("pool_steps"))

            def rstd(sem, count, src, dst, n, scale, done):
                pool.wait_ge(sem, count)
                own(nc.gpsimd.tensor_scalar(dst, src, scale, EPS, ALU.mult, ALU.add))
                own.sync()
                nc.gpsimd.tensor_tensor(dst, dst, neghalf[:, 0:n], ALU.pow).then_inc(done, 1)

            def rs(name):
                return st[:, 2 * (RS_AT + SS[name]):2 * (RS_AT + SS[name]) + 2]

            own(nc.gpsimd.memset(neghalf, -0.5))
            own(nc.gpsimd.memset(hQ[:, :, :].rearrange("p a b -> p (a b)"), 0.0))
            own(nc.gpsimd.memset(hK[:, :, :].rearrange("p a b -> p (a b)"), 0.0))
            own.sync()
            nc.gpsimd.memset(ones, 1.0).then_inc(S("ones_set"), 1)
            own.sync()
            rstd(S("squares"), squared("mix"), s_(SS["mix"]), rs("mix"), 2, 1.0 / D, S("roots"))
            for n in range(R):
                lo(n, n + 1)
            los(R, T_WOUT)

            kf, qf, bf = (t_.rearrange("p a b -> p (a b)") for t_ in (hk, hq, hb))

            def level_diff(l):
                h = LEVELS[l]
                if l >= 2:
                    pool.wait_ge(S("h_qk"), l - 1)
                g_ = bf.rearrange("p (a n) -> p a n", n=2 * h)
                nc.gpsimd.tensor_tensor(hdec[:, l % 2, :].rearrange("p (a n) -> p a n", n=2 * h), g_,
                    g_[:, :, h - 1:h].to_broadcast([P, 256 // h, 2 * h]), ALU.subtract).then_inc(S("h_diff"), 1)

            def level_qk(l):
                h = LEVELS[l]
                pool.wait_ge(S("h_dec"), l + 1)
                if l >= 2:
                    pool.wait_ge(S("h_sc"), 2 * l)
                sh = "p (a two h) -> p a two h"
                d_, k_, q_, K_, Q_ = (t_.rearrange(sh, two=2, h=h) for t_ in
                                      (hdec[:, l % 2, :], kf, qf, hK[:, l % 2, :], hQ[:, l % 2, :]))
                nc.gpsimd.tensor_tensor(K_[:, :, 0, :], k_[:, :, 0, :], d_[:, :, 0, :], ALU.mult)
                nc.gpsimd.tensor_tensor(Q_[:, :, 1, :], q_[:, :, 1, :], d_[:, :, 1, :], ALU.mult).then_inc(S("h_qk"), 1)

            pool.wait_ge(S("hb_done"), 1)
            level_diff(0)
            level_diff(1)
            for l in range(7):
                level_qk(l)
                if l + 2 < 7:
                    level_diff(l + 2)
                if l == 5:
                    pool.wait_ge(S("h_qk"), 6)
                    nc.gpsimd.tensor_tensor(hdec[:, 1, 0:256].rearrange("p (c t) -> p c t", c=2), hb[:, :, 0:P],
                                            hb[:, :, P - 1:P].to_broadcast([P, 2, P]), ALU.subtract)\
                        .then_inc(S("h_diff"), 1)
            pool.wait_ge(S("h_dec"), 8)
            x_ = hdec[:, 1, :].rearrange("p (s c t) -> p s c t", s=2, c=2)
            nc.gpsimd.tensor_tensor(x_[:, 0], x_[:, 0], hk[:, :, 0:P], ALU.mult)
            nc.gpsimd.tensor_tensor(x_[:, 1], x_[:, 1], hq[:, :, P:T], ALU.mult).then_inc(S("h_qk"), 1)
            for n in range(T_WOUT, T_WOUT + R):
                lo(n % R, n + 1)
            rstd(S("squares"), squared("lru"), s_(SS["lru"]), rs("lru"), 2, 1.0 / 256, S("roots"))
            rstd(S("squares"), squared("att"), s_(SS["att"]), rs("att"), 2, 1.0 / 512, S("roots"))
            rstd(S("hg_ss"), 1, hss, hrs, 8, 1.0 / 64, S("roots"))
            los(T_WOUT + R, T_FFN + R)
            rstd(S("squares"), squared("mlp"), s_(SS["mlp"]), rs("mlp"), 2, 1.0 / D, S("roots"))
            los(T_FFN + R, T_IN2_F + R)
            rstd(S("squares"), squared("fin"), s_(SS["fin"]), rs("fin"), 2, 1.0 / D, S("roots"))
            rstd(S("squares"), squared("in2"), s_(SS["n1"]), rs("n1"), 2, 1.0 / D, S("roots"))
            los(T_IN2_F + R, T_IN2_M + 16 + R)
            rstd(S("squares"), squared("sgv"), s_(SS["sgv"]), rs("sgv"), 2, 1.0 / D, S("roots"))
            los(T_IN2_M + 16 + R, T_IN2_M + 44 + R)
            rstd(S("gla_ss"), 8, gss, grs, 8, 1.0 / 256, S("roots"))
            los(T_IN2_M + 44 + R, T_WOUT2 + R)
            los(T_WOUT2 + R, T_WQ + R)
            rstd(S("squares"), squared("wq"), s_(SS["n2"]), rs("n2"), 2, 1.0 / D, S("roots"))
            los(T_WQ + R, T_END)
            rstd(S("squares"), squared("last"), s_(SS["last"]), rs("last"), 2, 1.0 / D, S("roots"))

        @block.scalar
        def _(act):
            def hi(slot, group, used):
                act.wait_ge(raw_full[slot], group * 16 + 16)
                if used is not None:
                    act.wait_ge(tile_used, used)
                nc.scalar.activation(whi[:, slot, :], raw[:, slot, :], ACT.Copy).then_inc(hi_done, 1)

            def his(a, b):
                with act.Fori(0, (b - a) // R) as i:
                    for u in range(R):
                        hi((a + u) % R, i + (a + u) // R, i * R + (a + u + 1 - R))

            own = Steps(act, S("act_steps"))

            def sums(src, tt, n, scratch, dst, done):
                nc.scalar.activation(scratch[:, tt, 0:n], src, ACT.Square, accum_out=dst[:, tt:tt + 1])\
                    .then_inc(done, 1)

            def upper(name):
                for b in range(4):
                    act.wait_ge(S("turned_xg"), turn(name, 4, b + 1))
                    nc.scalar.activation(xh[:, 2 * b:2 * b + 2, :], xg[:, 2 * b:2 * b + 2, :], ACT.Copy)\
                        .then_inc(S("turned_hi"), 1)

            for tt in range(TT):
                act.wait_ge(S(f"x_in{tt}"), 16)
                sums(xres[:, tt, :], tt, D, xn, s_(SS["mix"]), S("squares"))
            for n in range(R):
                hi(n, 0, None)
            upper("mix")
            act.wait_ge(S("col_in"), 16)
            nc.scalar.activation(sil, c_("c"), ACT.Sigmoid).then_inc(S("sil_sig"), 1)
            act.wait_ge(S("lam_abs"), 1)
            nc.scalar.activation(tiny[:, 0:2], tiny[:, 0:2], ACT.Exp, scale=-1.0).then_inc(S("lam_exp"), 1)
            def upper_of(a, b):
                for n in range(a, b):
                    hi(n % R, n // R, n + 1 - R)

            his(R, T_IN_M + R)
            act.wait_ge(S("in_f"), 16)
            nc.scalar.activation(hk, zF[:, 6:8, :], ACT.Sigmoid, scale=-1.0).then_inc(S("hk_done"), 1)
            nc.scalar.activation(hq, zF[:, 4:6, :], ACT.Sigmoid).then_inc(S("hq_sig"), 1)
            upper_of(T_IN_M + 4, T_IN_M + 5)
            act.wait_ge(S("gy_arg"), 1)
            nc.scalar.activation(ld, gy, ACT.Sigmoid, scale=2.0 * 0.7978845608028654).then_inc(S("gy_sig"), 1)
            upper_of(T_IN_M + 5, T_IN_M + 6)
            act.wait_ge(S("lru_gates"), 1)
            for c in range(2):
                nc.scalar.activation(ri[:, c, :], bank[4][:, c * T:(c + 1) * T], ACT.Sigmoid, bias=c_("ba", c))
            for c in range(2):
                last = nc.scalar.activation(ri[:, 2 + c, :], bank[5][:, c * T:(c + 1) * T], ACT.Sigmoid,
                                            bias=c_("bx", c))
            last.then_inc(S("ri_done"), 1)
            for k, src in enumerate((h1, h2)):
                upper_of(T_IN_M + 6 + k, T_IN_M + 7 + k)
                act.wait_ge(S("hf_abs"), k + 1)
                own(nc.scalar.activation(src, src, ACT.Exp, scale=-1.0))
                own.sync()
                nc.scalar.activation(src, src, ACT.Ln, bias=1.0).then_inc(S("hf_ln"), 1)
            def level_dec(l):
                act.wait_ge(S("h_diff"), l + 1)
                if l == 7:
                    nc.scalar.activation(hdec[:, 1, 0:256], hdec[:, 1, 0:256], ACT.Exp, scale=-1.0)
                    nc.scalar.activation(hdec[:, 1, 256:512].rearrange("p (c t) -> p c t", c=2), hb[:, :, P:T],
                                         ACT.Exp).then_inc(S("h_dec"), 1)
                else:
                    d = hdec[:, l % 2, :].rearrange("p (a two h) -> p a two h", two=2, h=LEVELS[l])
                    nc.scalar.activation(d[:, :, 0, :], d[:, :, 0, :], ACT.Exp, scale=-1.0)
                    nc.scalar.activation(d[:, :, 1, :], d[:, :, 1, :], ACT.Exp).then_inc(S("h_dec"), 1)

            def head_exp(h):
                act.wait_ge(S("a_max"), h + 1)
                if h >= 2:
                    act.wait_ge(S("a_tr"), h - 1)
                for tt, (a, b) in enumerate(((0, 128), (128, 384))):
                    last = nc.scalar.activation(pp[:, h % 2, a:b], sc[:, h % 2, a:b], ACT.Exp,
                                                bias=nmx[:, 2 * h + tt:2 * h + tt + 1], scale=-1.0,
                                                accum_out=psm[:, 2 * h + tt:2 * h + tt + 1])
                last.then_inc(S("a_exp"), 1)

            level_dec(0)
            for h in range(8):
                if h < 7:
                    level_dec(h + 1)
                head_exp(h)
                if h == 2:
                    act.wait_ge(S("la_done"), 1)
                    nc.scalar.activation(lb_, la, ACT.Exp)
                    nc.scalar.activation(lc, la, ACT.Tanh).then_inc(S("a_done"), 1)
                if h == 4:
                    act.wait_ge(S("lru_m2"), 1)
                    nc.scalar.activation(lc, lc, ACT.Sqrt, scale=-1.0).then_inc(S("lru_sqrt"), 1)
                if h >= 6:
                    upper_of(T_WOUT + 2 * (h - 6), T_WOUT + 2 * (h - 5))
            nc.scalar.activation(sg, zM[:, :, 256:512], ACT.Sigmoid).then_inc(S("sg_sig"), 1)
            for tt in range(TT):
                act.wait_ge(S("lru_y"), 1)
                sums(y[:, tt, 0:256], tt, 256, xn, s_(SS["lru"]), S("squares"))
            act.wait_ge(S("att_y"), 2)
            act.wait_ge(S("squares"), squared("lru"))
            for tt in range(TT):
                sums(y[:, tt, 512:1024], tt, 512, xn, s_(SS["att"]), S("squares"))
            upper("y")
            his(T_WOUT + R, T_FFN + R)

            for tt in range(TT):
                act.wait_ge(S("x1_done"), 2 * tt + 2)
                sums(xres[:, tt, :], tt, D, xn, s_(SS["mlp"]), S("squares"))
            upper("mlp")

            def unit(slot, used, freed, func, done):
                act.wait_ge(tile_used, used)
                if freed is not None:
                    act.wait_ge(S(done + "_lo"), freed)
                nc.scalar.activation(ua[:, slot, :], bank[4 + slot][:, 0:T], func).then_inc(S(done + "_act"), 1)

            def units(base, count, func, name):
                def his_of(i, n0):
                    for n in (base + 3 + n0 * 2, base + 4 + n0 * 2):
                        hi(n % R, i + n // R if i is not None else n // R,
                           i * R + (n + 1 - R) if i is not None else n + 1 - R)

                unit(0, base + 1, None, func, name)
                hi((base + 4) % R, (base + 4) // R, base + 1)
                unit(1, base + 2, None, func, name)
                his_of(None, 1)
                with act.Fori(0, (count - 2) // 2) as j:
                    for u in range(2):
                        unit(u, j * 4 + (base + 4 + 2 * u), j * 2 + (u + 1), func, name)
                        his_of(j, 2 + u)
                n = base + 2 * count + 3
                hi(n % R, n // R, n + 1 - R)

            units(T_FFN, N_FFN, ACT.Relu, "ffn")

            for tt in range(TT):
                act.wait_ge(S("x2_done"), 2 * tt + 2)
                sums(xres[:, tt, :], tt, D, xn, s_(SS["fin"]), S("squares"))
            act.wait_ge(S("squares"), squared("fin"))
            for tt in range(TT):
                act.wait_ge(S("fin_done"), tt + 1)
                sums(xres[:, tt, :], tt, D, xn, s_(SS["n1"]), S("squares"))
            upper("in2")

            def read_out(group, tiles_end, dst, func, sum_to=None):
                for b in range(4):
                    if b < 3:
                        act.wait_ge(acc_ready, acc_filled(group, b))
                    else:
                        act.wait_ge(tile_used, tiles_end)
                    extra = {} if sum_to is None else dict(accum_out=sum_to[:, b:b + 1])
                    last = nc.scalar.activation(dst[:, b // 2, (b % 2) * 512:(b % 2 + 1) * 512], bank[b][:, :],
                                                func, **extra)
                    last.then_inc(S(READ_OUT[group]), 1)

            for n in range(T_IN2_F + R, T_IN2_F + R + 3):
                hi(n % R, n // R, n + 1 - R)
            his(T_IN2_F + R + 3, T_IN2_M + 8 + 3)
            read_out("m_sv", T_IN2_M + 8, msv, ACT.Gelu, st[:, 2 * SS["sgs"]:2 * SS["sgs"] + 4])
            act.wait_ge(S("sg_mean"), 1)
            for tt in range(TT):
                nc.scalar.activation(xn[:, tt, :], msv[:, tt, :], ACT.Square, bias=s_(SS["sgm"])[:, tt:tt + 1],
                                     accum_out=s_(SS["sgv"])[:, tt:tt + 1]).then_inc(S("squares"), 1)
            his(T_IN2_M + 8 + 3, T_IN2_M + 16 + 3)
            read_out("m_su", T_IN2_M + 16, msu, ACT.Gelu)
            act.wait_ge(S("z_abs"), 1)
            own(nc.scalar.activation(t1, t1, ACT.Exp, scale=-1.0))
            own.sync()
            nc.scalar.activation(t1, t1, ACT.Ln, bias=1.0).then_inc(S("z_ln"), 1)
            his(T_IN2_M + 16 + 3, T_IN2_M + 24 + 3)
            act.wait_ge(S("g_diff"), 1)
            nc.scalar.activation(t2, t1, ACT.Exp, scale=1.0 / 16)
            nc.scalar.activation(t3, t1, ACT.Exp, scale=-1.0 / 16).then_inc(S("g_dec"), 1)
            act.wait_ge(S("g_diffx"), 1)
            nc.scalar.activation(t1[:, :, 0:P], t1[:, :, 0:P], ACT.Exp, scale=-1.0 / 16)
            nc.scalar.activation(t1[:, :, P:T], tG[:, :, P:T], ACT.Exp, scale=1.0 / 16).then_inc(S("g_dec"), 1)
            his(T_IN2_M + 24 + 3, T_IN2_M + 32 + 3)
            act.wait_ge(S("r_out"), 4)
            nc.scalar.activation(xn, mr, ACT.Sigmoid).then_inc(S("r_sig"), 1)
            his(T_IN2_M + 32 + 3, T_IN2_M + 40 + 3)
            read_out("m_ga", T_IN2_M + 40, mga, ACT.Sigmoid)
            act.wait_ge(S("r_gated"), 1)
            act.wait_ge(S("gla_o"), 1)
            for tt in range(TT):
                for h in range(4):
                    nc.scalar.activation(xn[:, tt, h * T:(h + 1) * T],
                                         bank[4 + 2 * tt + h // 2][:, (h % 2) * T:(h % 2 + 1) * T], ACT.Square,
                                         accum_out=gss[:, 4 * tt + h:4 * tt + h + 1]).then_inc(S("gla_ss"), 1)
            his(T_IN2_M + 40 + 3, T_IN2_M + 48 + 3)
            read_out("m_gb", T_IN2_M + 48, mgb, ACT.Sigmoid)
            hi((T_WOUT2 + 3) % R, (T_WOUT2 + 3) // R, T_WOUT2)
            upper("merged")
            his(T_WOUT2 + R, T_WQ + R)
            for tt in range(TT):
                act.wait_ge(S("x3_done"), 2 * tt + 2)
                sums(xres[:, tt, :], tt, D, xn, s_(SS["n2"]), S("squares"))
            upper("wq")
            his(T_WQ + R, T_PEER + R)
            act.wait_ge(S("spilled"), 32)

            def expert_units(c, i):
                k = i * R if i is not None else 0
                act.wait_ge(tile_used, k + (T_PEER + c + 1))
                dst = arena[:, c * T:(c + 1) * T] if i is None else arena[:, bass.ds(i * (R * T) + c * T, T)]
                nc.scalar.activation(dst, bank[4 + c % 2][:, 0:T], ACT.Gelu).then_inc(S("expert_act"), 1)
                n = T_PEER + c + R
                hi(n % R, (i + n // R) if i is not None else n // R, k + (n + 1 - R))

            EXP_AT = 44
            with act.Fori(0, EXP_AT // R) as i:
                for u in range(R):
                    expert_units(u, i)
            act.wait_ge(S("top_shift"), 1)
            nc.scalar.activation(tg, tg, ACT.Exp).then_inc(S("top_exp"), 1)
            with act.Fori(0, (HALF - EXP_AT) // R) as i:
                for u in range(R):
                    expert_units(EXP_AT + u, i)
            act.wait_ge(S("weighted"), 2)
            with act.Fori(0, HALF // R) as i:
                for u in range(R):
                    expert_units(HALF + u, i)

            def expert_upper(c, i, ahead=True):
                k = i * R if i is not None else 0
                if not (c < 2 and i is None):
                    act.wait_ge(tile_used, k + (T_UP + c - 1))
                src = arena[:, c * T:(c + 1) * T] if i is None else arena[:, bass.ds(i * (R * T) + c * T, T)]
                nc.scalar.activation(uh[:, c % 2, :], src, ACT.Copy).then_inc(S("u_hi"), 1)
                n = T_UP + c + 2
                if ahead and n >= T_UP + R:
                    hi(n % R, (i + n // R) if i is not None else n // R, k + (n + 1 - R))

            act.wait_ge(S("weighted"), 2 + HALF)
            for c in range(R):
                expert_upper(c, None)
            with act.Fori(0, HALF // R - 1) as i:
                for u in range(R):
                    expert_upper(R + u, i)
            act.wait_ge(S("weighted"), 2 + N_PEER)
            with act.Fori(0, HALF // R - 1) as i:
                for u in range(R):
                    expert_upper(HALF + u, i)
            for c in range(N_PEER - R, N_PEER):
                expert_upper(c, None, ahead=c + 2 < N_PEER)
            for tt in range(TT):
                act.wait_ge(S("x4_done"), 2 * tt + 2)
                sums(xres[:, tt, :], tt, D, fin_o, s_(SS["last"]), S("squares"))

        @block.tensor
        def _(pe):
            def f_tile(slot, count, dst, turned=None):
                pe.wait_ge(lo_done, count)
                for k in range(KC):
                    if turned and k % 2 == 0:
                        pe.wait_ge(S("turned_lo"), turn(turned, 4, k // 2 + 1))
                    h_, l_ = whi[:, slot, k * P:(k + 1) * P], wlo[:, slot, k * P:(k + 1) * P]
                    nc.tensor.matmul(dst, h_, xh[:, k, :], start=(k == 0), stop=False)
                    nc.tensor.matmul(dst, h_, xl[:, k, :], start=False, stop=False)
                    last = nc.tensor.matmul(dst, l_, xh[:, k, :], start=False, stop=(k == KC - 1))
                last.then_inc(tile_used, 1)

            def m_tile(slot, count, ah, al, group=None, start=False, final=False):
                pe.wait_ge(lo_done, count)
                start = start or group is not None
                for b in range(4):
                    tt, half = b // 2, b % 2
                    cs = slice(half * 512, (half + 1) * 512)
                    ts = slice(tt * P, (tt + 1) * P)
                    if group is not None:
                        name, n = acc_freed(group, b)
                        pe.wait_ge(S(name), n)
                    nc.tensor.matmul(bank[b][:, :], ah[:, ts], whi[:, slot, cs], start=start, stop=False)
                    nc.tensor.matmul(bank[b][:, :], ah[:, ts], wlo[:, slot, cs], start=False, stop=False)
                    last = nc.tensor.matmul(bank[b][:, :], al[:, ts], whi[:, slot, cs], start=False, stop=final)
                    if b == 3:
                        last.then_inc(tile_used, 1)
                    elif final:
                        last.then_inc(acc_ready, 1)

            def m_group(a, group, turned=None, fourth=lambda: None):
                for k in range(KC):
                    if k == 3:
                        fourth()
                    if turned and k % 2 == 0:
                        pe.wait_ge(S("turned_lo"), turn(turned, 4, k // 2 + 1))
                    m_tile((a + k) % R, a + k + 1, xh[:, k, :], xl[:, k, :], group if k == 0 else None, final=(k == KC - 1))

            def transposes(group, name, src):
                pe.wait_ge(S("unturned"), turn(name, 2, 2))
                for b in range(4):
                    freed = acc_freed(group, b)
                    if freed:
                        pe.wait_ge(S(freed[0]), freed[1])
                    for j in range(2):
                        for tt in range(TT):
                            k = 2 * b + j
                            last = nc.tensor.transpose(bank[b][:, j * T + tt * P:j * T + (tt + 1) * P],
                                                       src[:, tt, k * P:(k + 1) * P], ident[:, :])
                    last.then_inc(acc_ready, 1)

            pe.wait_ge(S("ident_in"), 16)
            transposes("mix_T", "mix", xn)
            for n in range(2):
                f_tile(n, n + 1, bank[4 + n][:, 0:T], None if n else "mix")
            for n in range(2, R):
                pe.wait_ge(S("in_f"), n - 1)
                f_tile(n, n + 1, bank[4 + n % 2][:, 0:T])
            with pe.Fori(0, N_IN_F // R - 1) as i:
                for u in range(R):
                    pe.wait_ge(S("in_f"), i * R + (R + u - 1))
                    f_tile(u, i * R + (R + u + 1), bank[4 + u % 2][:, 0:T])
            def lru_gates():
                pe.wait_ge(S("consts1_in"), 64)
                pe.wait_ge(S("xc_done"), 1)
                for g in range(2):
                    for c in range(2):
                        for b in range(2):
                            ps = slice(64 * b, 64 * b + 64)
                            last = nc.tensor.matmul(bank[4 + g][ps, c * T:(c + 1) * T], lw[ps, 2 * g + c, :],
                                                    xc[ps, c, :], start=True, stop=True)
                last.then_inc(S("lru_gates"), 1)

            m_group(T_IN_M, "in_M", fourth=lru_gates)

            ada_at = [0]

            def ada_tiles(count):
                for n in range(ada_at[0], ada_at[0] + count):
                    g, m = n // 4, n % 4
                    ring = adar if n < ADA_FIRST else adar2
                    pe.wait_ge(ada_full[n % R], 16 * (n // R + 1))
                    if m == 0 and g >= 2:
                        pe.wait_ge(S("ada_out"), g - 1)
                    for j in range(2):
                        k = 2 * m + j
                        last = nc.tensor.matmul(bank[6 + g % 2][:, :], sil[:, k:k + 1].to_broadcast([P, P]),
                                                ring[:, n % R, j * 512:(j + 1) * 512],
                                                start=(k == 0), stop=(k == KC - 1))
                    last.then_inc(ada_used, 1)
                ada_at[0] += count

            def a_scores(h):
                ps = slice(64 * (h % 2), 64 * (h % 2) + 64)
                if h:
                    pe.wait_ge(S("a_max"), h)
                q_, k_ = zF[ps, 8 + h // 2, :], zF[ps, 12 + h // 2, :]
                nc.tensor.matmul(bank[3][:, 0:128], q_[:, 0:P], k_[:, 0:P], start=True, stop=True)
                nc.tensor.matmul(bank[3][:, 128:384], q_[:, P:T], k_, start=True, stop=True)\
                    .then_inc(S("a_sc"), 1)

            def a_turn(h):
                pe.wait_ge(S("a_exp"), h + 1)
                if h:
                    pe.wait_ge(S("a_pT"), h)
                for j in range(3):
                    last = nc.tensor.transpose(bank[2][:, j * P:(j + 1) * P], pp[:, h % 2, j * P:(j + 1) * P],
                                               ident[:, :])
                last.then_inc(S("a_tr"), 1)

            def a_values(h):
                pe.wait_ge(S("a_pT"), h + 1)
                v_ = slice(512 + 64 * h, 512 + 64 * h + 64)
                o_ = slice(64 * h, 64 * h + 64)
                nc.tensor.matmul(bank[0][:, o_], pT[:, h % 2, 0:128], zM[:, 0, v_], start=True, stop=True)
                nc.tensor.matmul(bank[1][:, o_], pT[:, h % 2, 128:256], zM[:, 0, v_], start=True, stop=False)
                nc.tensor.matmul(bank[1][:, o_], pT[:, h % 2, 256:384], zM[:, 1, v_], start=False, stop=True)\
                    .then_inc(S("a_o"), 1)

            def level_scores(l):
                if l:
                    pe.wait_ge(S("h_qk"), l)
                else:
                    pe.wait_ge(S("hb_done"), 1)
                if l == 0:
                    pe.wait_ge(S("ri_done"), 1)
                else:
                    pe.wait_ge(S("h_acc"), 2 * l)
                if l == 8:
                    for c in range(2):
                        for odd in range(2):
                            ps = slice(64 * odd, 64 * odd + 64)
                            cs = slice(c * P, (c + 1) * P)
                            last = nc.tensor.matmul(bank[4 + odd][:, cs], hdec[ps, 1, 0:256][:, cs],
                                                    hdec[ps, 1, 256:512][:, cs], start=True, stop=True)
                            if c:
                                last.then_inc(S("h_sc"), 1)
                    return
                src_k, src_q = (hK[:, (l - 1) % 2, :], hQ[:, (l - 1) % 2, :]) if l else \
                    (hk.rearrange("p a b -> p (a b)"), hq.rearrange("p a b -> p (a b)"))
                for n in range(4):
                    tt, c = n // 2, n % 2
                    for odd in range(2):
                        ps = slice(64 * odd, 64 * odd + 64)
                        cs = slice(c * T + tt * P, c * T + (tt + 1) * P)
                        last = nc.tensor.matmul(bank[4 + odd][:, n * P:(n + 1) * P], src_k[ps, cs],
                                                src_q[ps, cs], start=True, stop=True)
                        if n == 3:
                            last.then_inc(S("h_sc"), 1)

            pe.wait_ge(S("in_m"), 4)
            a_scores(0)
            pe.wait_ge(S("sil_done"), 1)
            ada_tiles(2)
            for l in range(9):
                level_scores(l)
                if l + 1 < 8:
                    a_scores(l + 1)
                if l:
                    a_values(l - 1)
                if l < 8:
                    a_turn(l)
                ada_tiles(l % 2)
            pe.wait_ge(S("lru_h"), 1)
            for tt in range(TT):
                for c in range(2):
                    last = nc.tensor.transpose(bank[3][:, tt * T + c * P:tt * T + (c + 1) * P],
                                               xc[:, c, tt * P:(tt + 1) * P], ident[:, :])
            last.then_inc(S("lru_tr"), 1)
            pe.wait_ge(S("h_acc"), 18)
            for tt in range(TT):
                for h in range(4):
                    dst = bank[5][:, tt * T + h * 64:tt * T + (h + 1) * 64]
                    last = nc.tensor.matmul(dst, att[:, 4 * (h % 2) + 2 * tt + h // 2, :], zM[:, tt, h * 64:(h + 1) * 64],
                                            start=True, stop=(tt == 0))
                    if tt:
                        last = nc.tensor.matmul(dst, attx[:, 2 * (h % 2) + h // 2, :], zM[:, 0, h * 64:(h + 1) * 64],
                                                start=False, stop=True)
            last.then_inc(S("h_o"), 1)
            ada_tiles(10 - ada_at[0])
            transposes("y_T", "y", y)
            ada_tiles(2)
            m_group(T_WOUT, "wout", "y")

            ada_tiles(4)
            transposes("mlp_T", "mlp", xn)
            ada_tiles(4)

            def pairs(base, count, group, name, name_of_turn):
                def m_of(slot, count_, u, ready, **kw):
                    pe.wait_ge(S(name + "_lo"), ready)
                    m_tile(slot, count_, uh[:, u, :], ul[:, u, :], **kw)

                f_tile(base % R, base + 1, bank[4][:, 0:T], name_of_turn)
                f_tile((base + 1) % R, base + 2, bank[5][:, 0:T])
                m_of((base + 2) % R, base + 3, 0, 1, group=group)
                with pe.Fori(0, (count - 2) // 2) as j:
                    for u in range(2):
                        pe.wait_ge(S(name + "_act"), j * 2 + (1 + u))
                        f_tile((base + 3 + 2 * u) % R, j * 4 + (base + 4 + 2 * u), bank[4 + u][:, 0:T])
                        m_of((base + 4 + 2 * u) % R, j * 4 + (base + 5 + 2 * u), (1 + u) % 2, j * 2 + (2 + u))
                n = base + 2 * count - 1
                m_of(n % R, n + 1, (count - 1) % 2, count, final=True)

            pairs(T_FFN, N_FFN, "ffn", "ffn", "mlp")
            ada_tiles(8)

            transposes("in2_T", "in2", xn)
            ada_tiles(4)
            for n in range(2):
                f_tile((T_IN2_F + n) % R, T_IN2_F + n + 1, bank[4 + n][:, 0:T], None if n else "in2")
            for n in range(2, N_IN2_F):
                pe.wait_ge(S("qk_out"), n - 1)
                f_tile((T_IN2_F + n) % R, T_IN2_F + n + 1, bank[4 + n % 2][:, 0:T])
            pe.wait_ge(S("ada_out"), 8)
            pe.wait_ge(S("consts2_in"), 96)
            for k in range(KC):
                last = nc.tensor.matmul(bank[6][0:16, 0:T], wal[:, k, :], xg[:, k, :], start=(k == 0),
                                        stop=(k == KC - 1))
            last.then_inc(S("alr"), 1)
            m_group(T_IN2_M, "m_sv")
            pe.wait_ge(S("alr_out"), 1)
            for h in range(4):
                last = nc.tensor.matmul(bank[6 + h // 2][:, (h % 2) * T:(h % 2 + 1) * T], wupt[:, h * P:(h + 1) * P],
                                        alT, start=True, stop=True)
            last.then_inc(S("z_mm"), 1)
            m_group(T_IN2_M + 8, "m_su")
            m_group(T_IN2_M + 16, "m_v")
            pe.wait_ge(S("sgw_masked"), 1)
            pe.wait_ge(S("sv_done"), 2)
            for tt in range(TT):
                for g in range(8):
                    last = nc.tensor.matmul(bank[4 + 2 * tt + g // 4][:, (g % 4) * P:(g % 4 + 1) * P], sgw[:, g, :],
                                            msv[:, tt, g * P:(g + 1) * P], start=True, stop=True)
                    if g % 4 == 3:
                        last.then_inc(S("sgu_mm"), 1)
            m_group(T_IN2_M + 24, "m_r")
            pe.wait_ge(S("sgu_done"), 4)
            pe.wait_ge(S("g_qk"), 2)
            for tt in range(TT):
                for h in range(4):
                    last = nc.tensor.matmul(bank[4 + tt][:, h * P:(h + 1) * P], t3[:, h, tt * P:(tt + 1) * P],
                                            t2[:, h, tt * P:(tt + 1) * P], start=True, stop=True)
                last.then_inc(S("g_sc"), 1)
            for h in range(4):
                last = nc.tensor.matmul(bank[6][:, h * P:(h + 1) * P], t1[:, h, 0:P], t1[:, h, P:T],
                                        start=True, stop=True)
            last.then_inc(S("g_sc"), 1)
            m_group(T_IN2_M + 32, "m_ga")
            pe.wait_ge(S("g_at"), 3)
            for tt in range(TT):
                for h in range(4):
                    dst = bank[4 + 2 * tt + h // 2][:, (h % 2) * T:(h % 2 + 1) * T]
                    last = nc.tensor.matmul(dst, AT[:, 4 * tt + h, :], mv[:, tt, h * T:(h + 1) * T],
                                            start=True, stop=(tt == 0))
                    if tt:
                        last = nc.tensor.matmul(dst, AT[:, 8 + h, :], mv[:, 0, h * T:(h + 1) * T],
                                                start=False, stop=True)
            last.then_inc(S("gla_o"), 1)
            m_group(T_IN2_M + 40, "m_gb")
            pe.wait_ge(S("go_done"), 1)
            ada_tiles(4)
            transposes("merged_T", "merged", go)
            ada_tiles(4)
            m_group(T_WOUT2, "wout2", "merged")

            ada_tiles(4)
            transposes("wq_T", "wq", xn)
            ada_tiles(4)
            for n in range(2):
                f_tile((T_WQ + n) % R, T_WQ + n + 1, bank[4 + n][:, 0:T], None if n else "wq")
            for n in range(2, R):
                pe.wait_ge(S("pq_out"), n - 1)
                f_tile((T_WQ + n) % R, T_WQ + n + 1, bank[4 + n % 2][:, 0:T])
            with pe.Fori(0, N_WQ // R - 1) as i:
                for u in range(R):
                    pe.wait_ge(S("pq_out"), i * R + (R + u - 1))
                    f_tile(u, i * R + (T_WQ + R + u + 1), bank[4 + u % 2][:, 0:T])
            pe.wait_ge(S("keys_in"), 16)
            pe.wait_ge(S("pq_out"), 16)
            for q in range(8):
                if q >= 4:
                    pe.wait_ge(S("sc_out"), q - 3)
                for j in range(4):
                    n = 4 * q + j
                    tt, m = n // 16, n % 16
                    last = nc.tensor.matmul(bank[q % 4][:, j * P:(j + 1) * P], pq[:, m, tt * P:(tt + 1) * P],
                                            ky[:, m % 2, :], start=True, stop=True)
                last.then_inc(S("sc_mm"), 1)

            def expert_f(c, i):
                k = i * R if i is not None else 0
                if i is not None or c >= 2:
                    pe.wait_ge(S("expert_act"), k + (c - 1))
                f_tile(c % R, k + (T_PEER + c + 1), bank[4 + c % 2][:, 0:T])

            def weights4(q, i):
                k = i * R if i is not None else 0
                pe.wait_ge(S("onehot"), k + (q + 1))
                pe.wait_ge(S("weighted"), k + (q + 1))
                for t_ in range(4):
                    for part in range(3):
                        last = nc.tensor.matmul(bank[6 + q % 2][:, t_ * HALF:(t_ + 1) * HALF], oneB[:, q % 2, t_, :],
                                                oneA[:, q % 2, part, t_, :], start=(part == 0), stop=(part == 2))
                last.then_inc(S("weights_made"), 1)

            for c in range(R):
                expert_f(c, None)
            CHOSEN_AT = 56
            with pe.Fori(0, CHOSEN_AT // R - 1) as i:
                for u in range(R):
                    expert_f(R + u, i)
            pe.wait_ge(S("chosen"), 1)
            for j, src in enumerate((t1f, t2f, tg)):
                for tt in range(TT):
                    last = nc.tensor.transpose(bank[6 + j // 2][:, (j % 2) * T + tt * P:(j % 2) * T + (tt + 1) * P],
                                               src[:, 8 * tt:8 * tt + 8, :], ident[:, :])
            last.then_inc(S("chosen_T"), 1)
            with pe.Fori(0, (HALF - CHOSEN_AT) // R) as i:
                for u in range(R):
                    expert_f(CHOSEN_AT + u, i)
            with pe.Fori(0, HALF // R) as i:
                for u in range(R):
                    weights4(u, i)
                    expert_f(HALF + u, i)

            def expert_m(c, i, **kw):
                k = i * R if i is not None else 0
                pe.wait_ge(S("u_lo"), k + (c + 1))
                m_tile(c % R, k + (T_UP + c + 1), uh[:, c % 2, :], ul[:, c % 2, :], **kw)

            for c in range(R):
                weights4(HALF + c, None)
                expert_m(c, None, start=(c == 0))
            with pe.Fori(0, HALF // R - 1) as i:
                for u in range(R):
                    weights4(HALF + R + u, i)
                    expert_m(R + u, i)
            with pe.Fori(0, HALF // R - 1) as i:
                for u in range(R):
                    expert_m(HALF + u, i)
            for c in range(N_PEER - R, N_PEER):
                expert_m(c, None, final=(c == N_PEER - 1))

        @block.vector
        def _(v):
            own = Steps(v, S("dve_steps"))
            tst, tsc, ttt, stt = nc.vector.tensor_tensor, nc.vector.tensor_scalar, nc.vector.tensor_tensor, \
                nc.vector.scalar_tensor_tensor

            def rs(name, tt):
                a = 2 * (RS_AT + SS[name]) + tt
                return st[:, a:a + 1]

            def scaled(name, key):
                v.wait_ge(S("roots"), rooted(name))
                for tt in range(TT):
                    tsc(xn[:, tt, :], xres[:, tt, :], rs(key, tt), None, ALU.mult).then_inc(S("unturned"), 1)

            def turned(group, name, gains, shifts=None):
                def lower_part(b):
                    v.wait_ge(S("turned_hi"), turn(name, 4, b + 1))
                    ttt(xl[:, 2 * b:2 * b + 2, :], xg[:, 2 * b:2 * b + 2, :],
                        xh[:, 2 * b:2 * b + 2, :].bitcast(F32), ALU.subtract).then_inc(S("turned_lo"), 1)

                for b in range(4):
                    v.wait_ge(acc_ready, acc_filled(group, b))
                    for j in range(2):
                        k = 2 * b + j
                        src = bank[b][:, j * T:(j + 1) * T]
                        if gains is None:
                            ins = nc.vector.tensor_copy(xg[:, k, :], src)
                        elif shifts is None:
                            ins = tsc(xg[:, k, :], src, gains[:, k:k + 1], None, ALU.mult)
                        else:
                            ins = tsc(xg[:, k, :], src, gains[:, k:k + 1], shifts[:, k:k + 1], ALU.mult, ALU.add)
                        if j:
                            ins.then_inc(S("turned_xg"), 1)
                    if b:
                        lower_part(b - 1)
                lower_part(3)

            def ada_group(g):
                v.wait_ge(ada_used, 4 * (g + 1))
                if g >= 8:
                    v.wait_ge(S("gate1_b" if g < 10 else "gate2_b"), 16)
                    dst = (gate1 if g < 10 else gate2)[:, (g % 2) * 512:(g % 2 + 1) * 512]
                    ttt(dst, bank[6 + g % 2][:, :], dst, ALU.add).then_inc(S("ada_out"), 1)
                    return
                own.sync()
                diag = gate2[:, 0:512].rearrange("p (a b) -> p a b", a=4)
                ttt(diag, bank[6 + g % 2][:, :].rearrange("p (a b) -> p a b", a=4),
                    ident[:, :].unsqueeze(1).to_broadcast([P, 4, P]), ALU.mult).then_inc(S("ada_out"), 1)
                v.wait_ge(S("ada_out"), g + 1)
                own(nc.vector.tensor_reduce(mod[:, 4 * g:4 * g + 4], diag, AX.X, ALU.add)); own.sync()
                last = ttt(mod[:, 4 * g:4 * g + 4], mod[:, 4 * g:4 * g + 4], c_("bada", 4 * g, 4), ALU.add)
                last.then_inc(S("mod_done"), 1) if g == 7 else own(last)

            def filled(group, b, tiles_end):
                if b < 3:
                    v.wait_ge(acc_ready, acc_filled(group, b))
                else:
                    v.wait_ge(tile_used, tiles_end)

            v.wait_ge(S("col_in"), 16)
            stt(tiny[:, 0:2], c_("lam"), -1.0, c_("lam"), ALU.mult, ALU.max).then_inc(S("lam_abs"), 1)
            scaled("mix", "mix")
            turned("mix_T", "mix", c_("mix"))
            def chunks(a, n, dst, j0, done, scale=None):
                with v.Fori(0, n // 2) as i:
                    for u in range(2):
                        v.wait_ge(tile_used, i * 2 + (a + u + 1))
                        d_ = dst[:, bass.ds(i * 2 + (j0 + u), 1), :]
                        src = bank[4 + u][:, 0:T].unsqueeze(1)
                        if scale is None:
                            nc.vector.tensor_copy(d_, src).then_inc(done, 1)
                        else:
                            tsc(d_, src, scale, None, ALU.mult).then_inc(done, 1)

            z, s, s2, acc, m = (tiny[:, 2 * j:2 * j + 2] for j in range(5))

            def series(terms):
                for n in terms:
                    own(ttt(acc, acc, s2, ALU.mult)); own.sync()
                    own(tsc(acc, acc, 1.0 / n, None, ALU.add)); own.sync()

            chunks(T_IN_F, 4, zF, 0, S("in_f"))
            v.wait_ge(S("lam_exp"), 1)
            own(tsc(s2, z, 2.0, None, ALU.add)); own.sync()
            own(nc.vector.reciprocal(s2, s2)); own.sync()
            own(ttt(s, z, s2, ALU.mult)); own.sync()
            own(ttt(s2, s, s, ALU.mult)); own.sync()
            own(nc.vector.memset(acc, 1.0 / 17)); own.sync()
            chunks(T_IN_F + 4, 4, zF, 4, S("in_f"))
            series((15, 13, 11, 9))
            chunks(T_IN_F + 8, 4, zF, 8, S("in_f"), 0.125)
            series((7, 5, 3, 1))
            chunks(T_IN_F + 12, 4, zF, 12, S("in_f"))
            own(ttt(acc, acc, s, ALU.mult))
            own(tsc(m, c_("lam"), -1.0, 0.0, ALU.mult, ALU.max)); own.sync()
            own(stt(acc, acc, 2.0, m, ALU.mult, ALU.add)); own.sync()
            own(tsc(c8, acc, -8.0, None, ALU.mult))
            v.wait_ge(S("sil_sig"), 1)
            ttt(sil, sil, c_("c"), ALU.mult).then_inc(S("sil_done"), 1)
            v.wait_ge(S("in_f"), 16)

            for c in range(2):
                own(tsc(xc[:, c, :], zF[:, c, :], c_("convw", 4 * c + 3), c_("convb", c), ALU.mult, ALU.add))
            for j in (2, 1, 0):
                own.sync()
                for c in range(2):
                    last = stt(xc[:, c, 3 - j:T], zF[:, c, 0:T - 3 + j], c_("convw", 4 * c + j),
                               xc[:, c, 3 - j:T], ALU.mult, ALU.add)
                    if j:
                        own(last)
            last.then_inc(S("xc_done"), 1)
            own(ttt(gy, zF[:, 2:4, :], zF[:, 2:4, :], ALU.mult)); own.sync()
            own(tsc(gy, gy, 0.044715, 1.0, ALU.mult, ALU.add)); own.sync()
            ttt(gy, gy, zF[:, 2:4, :], ALU.mult).then_inc(S("gy_arg"), 1)
            f_ = zF[:, 6:8, :]
            stt(h1, f_, -1.0, f_, ALU.mult, ALU.max).then_inc(S("hf_abs"), 1)
            v.wait_ge(S("hq_sig"), 1)
            own(ttt(hq, hq, zF[:, 4:6, :], ALU.mult))
            v.wait_ge(S("gy_sig"), 1)
            own(ttt(gy, zF[:, 2:4, :], ld, ALU.mult))
            v.wait_ge(S("hf_ln"), 1)
            own(stt(h1, f_, 0.0, h1, ALU.min, ALU.subtract)); own.sync()
            own(tsc(hb, h1, LOG_TINY, None, ALU.subtract)); own.sync()
            stt(h2, hb, -1.0, hb, ALU.mult, ALU.max).then_inc(S("hf_abs"), 1)
            v.wait_ge(S("ri_done"), 1)
            for c in range(2):
                last = tsc(la[:, c, :], ri[:, c, :], c8[:, c:c + 1], None, ALU.mult)
            last.then_inc(S("la_done"), 1)
            for b in range(4):
                filled("in_M", b, T_WOUT)
                nc.vector.tensor_copy(zM[:, b // 2, (b % 2) * 512:(b % 2 + 1) * 512], bank[b][:, :])\
                    .then_inc(S("in_m"), 1)
            v.wait_ge(S("hf_ln"), 2)
            own(stt(h1, h1, LOG_TINY, h2, ALU.max, ALU.add)); own.sync()
            v.wait_ge(S("ones_set"), 1)
            v.wait_ge(S("hk_done"), 1)
            for c in range(2):
                for tt in range(TT):
                    ts = slice(tt * P, (tt + 1) * P)
                    last = nc.vector.tensor_tensor_scan(hb[:, c, ts], ones, h1[:, c, ts], 0.0, ALU.mult, ALU.add)
            last.then_inc(S("hb_done"), 1)
            v.wait_ge(S("consts1_in"), 64)
            def level_acc(l):
                for odd in range(2):
                    v.wait_ge(S("h_sc"), 2 * l + odd + 1)
                    if l:
                        v.wait_ge(S("h_acc"), 2 * (l - 1) + odd + 1)
                    src = bank[4 + odd][:, :].rearrange("p (a b) -> p a b", a=4)
                    dst = att[:, 4 * odd:4 * odd + 4, :]
                    mk = msk[:, l:l + 1, :].bitcast(U32).to_broadcast([P, 4, P])
                    if l:
                        nc.vector.copy_predicated(dst, mk, src).then_inc(S("h_acc"), 1)
                    else:
                        ttt(dst, src, ident[:, :].unsqueeze(1).to_broadcast([P, 4, P]), ALU.mult)\
                            .then_inc(S("h_acc"), 1)

            def a_soft(h):
                v.wait_ge(S("a_sc"), h + 1)
                if h >= 2:
                    v.wait_ge(S("a_exp"), h - 1)
                own(stt(sc[:, h % 2, :], ali, -2.0 ** -(h + 1), bank[3][:, 0:384], ALU.mult, ALU.subtract))
                own.sync()
                for tt, (a, b) in enumerate(((0, 128), (128, 384))):
                    last = nc.vector.tensor_reduce(nmx[:, 2 * h + tt:2 * h + tt + 1], sc[:, h % 2, a:b], AX.X, ALU.min)
                last.then_inc(S("a_max"), 1)

            def head_pT(h):
                v.wait_ge(S("a_tr"), h + 1)
                if h >= 2:
                    v.wait_ge(S("a_o"), h - 1)
                nc.vector.tensor_copy(pT[:, h % 2, :], bank[2][:, 0:384]).then_inc(S("a_pT"), 1)

            a_soft(0)
            for l in range(8):
                level_acc(l)
                if l + 1 < 8:
                    a_soft(l + 1)
                head_pT(l)
                if l == 3:
                    v.wait_ge(S("a_done"), 1)
                    own(ttt(la, lb_, lb_, ALU.mult)); own.sync()
                    own(ttt(ld, ri[:, 2:4, :], xc, ALU.mult))
                    stt(lc, la, 1.0, lc, ALU.add, ALU.mult).then_inc(S("lru_m2"), 1)
                if l == 5:
                    v.wait_ge(S("lru_sqrt"), 1)
                    own(ttt(ld, ld, lc, ALU.mult)); own.sync()
                    for c in range(2):
                        own(nc.vector.tensor_tensor_scan(la[:, c, :], lb_[:, c, :], ld[:, c, :], 0.0, ALU.mult, ALU.add))
                    own.sync()
                    ttt(xc, la, gy, ALU.mult).then_inc(S("lru_h"), 1)
                if l == 4:
                    ada_group(0)
            for odd in range(2):
                v.wait_ge(S("h_sc"), 17 + odd)
                nc.vector.tensor_copy(attx[:, 2 * odd:2 * odd + 2, :],
                                      bank[4 + odd][:, 0:T].rearrange("p (a b) -> p a b", a=2))\
                    .then_inc(S("h_acc"), 1)
            v.wait_ge(S("a_exp"), 8)
            own(nc.vector.reciprocal(prs, psm))
            v.wait_ge(S("lru_tr"), 1)
            nc.vector.tensor_copy(y[:, :, 0:256], bank[3][:, :].rearrange("p (a b) -> p a b", a=2))\
                .then_inc(S("lru_y"), 1)
            v.wait_ge(S("a_o"), 8)
            own.sync()
            for tt in range(TT):
                ttt(y[:, tt, 512:1024].rearrange("p (h e) -> p h e", h=8),
                    bank[tt][:, :].rearrange("p (h e) -> p h e", h=8),
                    prs.rearrange("p (h t) -> p h t", t=2)[:, :, tt:tt + 1].to_broadcast([P, 8, 64]),
                    ALU.mult).then_inc(S("att_y"), 1)
            v.wait_ge(S("sg_sig"), 1)
            own(ttt(sg, sg, zM[:, :, 256:512], ALU.mult))
            v.wait_ge(S("h_o"), 1)
            o_ = bank[5][:, :].rearrange("p (a b) -> p a b", a=2)
            own(nc.vector.tensor_copy(y[:, :, 256:512], o_)); own.sync()
            own(ttt(h1, y[:, :, 256:512], y[:, :, 256:512], ALU.mult)); own.sync()
            nc.vector.tensor_reduce(hss, h1.rearrange("p a (h e) -> p (a h) e", h=4), AX.X, ALU.add)\
                .then_inc(S("hg_ss"), 1)
            v.wait_ge(S("roots"), rooted("lru"))
            for tt in range(TT):
                own(tsc(y[:, tt, 0:256], y[:, tt, 0:256], rs("lru", tt), None, ALU.mult))
            v.wait_ge(S("roots"), rooted("hg"))
            v.wait_ge(S("roots"), rooted("att"))
            for tt in range(TT):
                yv = y[:, tt, 256:512].rearrange("p (h e) -> p h e", h=4)
                own(ttt(yv, yv, hrs[:, 4 * tt:4 * tt + 4].unsqueeze(2).to_broadcast([P, 4, 64]), ALU.mult))
            own.sync()
            own(ttt(y[:, :, 256:512], y[:, :, 256:512], sg, ALU.mult)); own.sync()
            for tt in range(TT):
                tsc(y[:, tt, 512:1024], y[:, tt, 512:1024], rs("att", tt), None, ALU.mult).then_inc(S("unturned"), 1)
            ada_group(1)
            turned("y_T", "y", c_("ygain"))
            ada_group(2)

            def add_to_x(group, tiles_end, done):
                for b in range(4):
                    filled(group, b, tiles_end)
                    xv = xres[:, b // 2, (b % 2) * 512:(b % 2 + 1) * 512]
                    ttt(xv, xv, bank[b][:, :], ALU.add).then_inc(S(done), 1)

            add_to_x("wout", T_FFN, "x1_done")
            scaled("mlp", "mlp")
            turned("mlp_T", "mlp", c_("mlp"))
            ada_group(3)
            ada_group(4)

            def split_units(slot, name, n, used):
                v.wait_ge(S(name + "_gated"), n)
                if used is not None:
                    v.wait_ge(tile_used, used)
                nc.vector.tensor_copy(uh[:, slot, :], ua[:, slot, :]).then_inc(S(name + "_uh"), 1)
                v.wait_ge(S(name + "_uh"), n)
                ttt(ul[:, slot, :], ua[:, slot, :], uh[:, slot, :].bitcast(F32), ALU.subtract)\
                    .then_inc(S(name + "_lo"), 1)

            def hidden(base, count, name, gate):
                for i in range(2):
                    v.wait_ge(S(name + "_act"), i + 1)
                    gate(i, i).then_inc(S(name + "_gated"), 1)
                    split_units(i, name, i + 1, None)
                with v.Fori(0, (count - 2) // 2) as j:
                    for u in range(2):
                        v.wait_ge(S(name + "_act"), j * 2 + (3 + u))
                        gate(u, j * 2 + (2 + u)).then_inc(S(name + "_gated"), 1)
                        split_units(u, name, j * 2 + (3 + u), j * 4 + (base + 3 + 2 * u))

            hidden(T_FFN, N_FFN, "ffn", lambda s_, i: ttt(ua[:, s_, :], ua[:, s_, :], ua[:, s_, :], ALU.mult))
            add_to_x("ffn", T_IN2_F, "x2_done")
            v.wait_ge(S("roots"), rooted("fin"))
            v.wait_ge(S("consts1_in"), 64)
            for tt in range(TT):
                stt(xres[:, tt, :], xres[:, tt, :], rs("fin", tt), tmp, ALU.mult, ALU.mult).then_inc(S("fin_done"), 1)

            ada_group(5)

            own(stt(gain[:, 0:8], mod[:, 8:16], 1.0, c_("n1"), ALU.add, ALU.mult))
            own.sync()
            v.wait_ge(S("fin_done"), 2)
            scaled("in2", "n1")
            turned("in2_T", "in2", gain[:, 0:8], mod[:, 0:8])
            for g in (6, 7):
                ada_group(g)
            v.wait_ge(S("mod_done"), 1)
            own(stt(gain[:, 8:16], mod[:, 24:32], 1.0, c_("n2"), ALU.add, ALU.mult))
            with v.Fori(0, 2) as i:
                for u in range(2):
                    v.wait_ge(tile_used, i * 2 + (T_IN2_F + u + 1))
                    tsc(qk[:, bass.ds(i * 2 + u, 1), :], bank[4 + u][:, 0:T].unsqueeze(1), 128 ** -0.5, None,
                        ALU.mult).then_inc(S("qk_out"), 1)
            chunks(T_IN2_F + 4, 4, qk, 4, S("qk_out"))
            v.wait_ge(S("alr"), 1)
            nc.vector.tensor_copy(alT, bank[6][0:16, 0:T]).then_inc(S("alr_out"), 1)

            def read_out(group, tiles_end, dst, done):
                for b in range(4):
                    filled(group, b, tiles_end)
                    nc.vector.tensor_copy(dst[:, b // 2, (b % 2) * 512:(b % 2 + 1) * 512], bank[b][:, :])\
                        .then_inc(S(done), 1)

            v.wait_ge(S("z_mm"), 1)
            for h in range(4):
                own(tsc(t2[:, h, :], bank[6 + h // 2][:, (h % 2) * T:(h % 2 + 1) * T], c_("balpha", h), None, ALU.add))
            own.sync()
            stt(t1, t2, -1.0, t2, ALU.mult, ALU.max).then_inc(S("z_abs"), 1)
            v.wait_ge(S("sv_out"), 4)
            sums = st[:, 2 * SS["sgs"]:2 * SS["sgs"] + 4].rearrange("p (a b) -> p a b", a=2)
            own(ttt(s_(SS["sgm"]).unsqueeze(2), sums[:, :, 0:1], sums[:, :, 1:2], ALU.add)); own.sync()
            tsc(s_(SS["sgm"]), s_(SS["sgm"]), -1.0 / D, None, ALU.mult).then_inc(S("sg_mean"), 1)
            v.wait_ge(S("consts2_in"), 96)
            ttt(sgw, sgw, caus.unsqueeze(1).to_broadcast([P, 8, P]), ALU.mult).then_inc(S("sgw_masked"), 1)
            v.wait_ge(S("roots"), rooted("sgv"))
            v.wait_ge(S("sg_mean"), 1)
            for tt in range(TT):
                own(tsc(msv[:, tt, :], msv[:, tt, :], s_(SS["sgm"])[:, tt:tt + 1], rs("sgv", tt), ALU.add, ALU.mult))
                own.sync()
                own(ttt(msv[:, tt, :], msv[:, tt, :], rw[:, 0, :], ALU.mult)); own.sync()
                ttt(msv[:, tt, :], msv[:, tt, :], rw[:, 1, :], ALU.add).then_inc(S("sv_done"), 1)
            v.wait_ge(S("z_ln"), 1)
            own(stt(t2, t2, 0.0, t1, ALU.min, ALU.subtract)); own.sync()
            for h in range(4):
                for tt in range(TT):
                    ts = slice(tt * P, (tt + 1) * P)
                    own(nc.vector.tensor_tensor_scan(tG[:, h, ts], ones, t2[:, h, ts], 0.0, ALU.mult, ALU.add))
            own.sync()
            v8 = lambda t_: t_.rearrange("p a (b c) -> p (a b) c", b=2)
            ttt(v8(t1), v8(tG), v8(tG)[:, :, 63:64].to_broadcast([P, 8, P]), ALU.subtract).then_inc(S("g_diff"), 1)
            read_out("m_v", T_IN2_M + 24, mv, "v_out")
            v.wait_ge(S("g_dec"), 1)
            ttt(t1[:, :, 0:P], tG[:, :, 0:P], tG[:, :, P - 1:P].to_broadcast([P, 4, P]), ALU.subtract)\
                .then_inc(S("g_diffx"), 1)
            ttt(t2, t2, qk[:, 0:4, :], ALU.mult)
            ttt(t3, t3, qk[:, 4:8, :], ALU.mult).then_inc(S("g_qk"), 1)
            v.wait_ge(S("g_dec"), 2)
            ttt(t1[:, :, 0:P], t1[:, :, 0:P], qk[:, 4:8, 0:P], ALU.mult)
            ttt(t1[:, :, P:T], t1[:, :, P:T], qk[:, 0:4, P:T], ALU.mult).then_inc(S("g_qk"), 1)
            for tt in range(TT):
                for g in range(8):
                    if g % 4 == 0:
                        v.wait_ge(S("sgu_mm"), 2 * tt + g // 4 + 1)
                    cs = slice(g * P, (g + 1) * P)
                    last = stt(msu[:, tt, cs], bank[4 + 2 * tt + g // 4][:, (g % 4) * P:(g % 4 + 1) * P],
                               c_("sgb", g), msu[:, tt, cs], ALU.add, ALU.mult)
                    if g % 4 == 3:
                        last.then_inc(S("sgu_done"), 1)
            read_out("m_r", T_IN2_M + 32, mr, "r_out")
            for tt in range(TT):
                v.wait_ge(S("g_sc"), tt + 1)
                ttt(AT[:, 4 * tt:4 * tt + 4, :], bank[4 + tt][:, :].rearrange("p (a b) -> p a b", a=4),
                    caus.unsqueeze(1).to_broadcast([P, 4, P]), ALU.mult).then_inc(S("g_at"), 1)
            v.wait_ge(S("g_sc"), 3)
            nc.vector.tensor_copy(AT[:, 8:12, :], bank[6][:, :].rearrange("p (a b) -> p a b", a=4))\
                .then_inc(S("g_at"), 1)
            v.wait_ge(S("r_sig"), 1)
            ttt(mr, mr, xn, ALU.mult).then_inc(S("r_gated"), 1)
            v.wait_ge(S("r_gated"), 1)
            own(ttt(mr, mr, gla_w.unsqueeze(1).to_broadcast([P, TT, D]), ALU.mult)); own.sync()
            v.wait_ge(S("ga_out"), 4)
            own(ttt(mr, mr, mga, ALU.mult)); own.sync()
            v.wait_ge(S("roots"), rooted("gla"))
            for tt in range(TT):
                for h in range(4):
                    n = 4 * tt + h
                    last = stt(go[:, tt, h * T:(h + 1) * T], bank[4 + 2 * tt + h // 2][:, (h % 2) * T:(h % 2 + 1) * T],
                               grs[:, n:n + 1], mr[:, tt, h * T:(h + 1) * T], ALU.mult, ALU.mult)
            last.then_inc(S("go_done"), 1)
            v.wait_ge(S("go_done"), 1)
            v.wait_ge(S("sgu_done"), 4)
            for b in range(4):
                tt, cs = b // 2, slice((b % 2) * 512, (b % 2 + 1) * 512)
                v.wait_ge(S("gb_out"), b + 1)
                own(ttt(msu[:, tt, cs], msu[:, tt, cs], mgb[:, tt, cs], ALU.mult)); own.sync()
                last = ttt(go[:, tt, cs], go[:, tt, cs], msu[:, tt, cs], ALU.add)
                last.then_inc(S("unturned"), 1) if b % 2 else own(last)
            ada_group(8)
            turned("merged_T", "merged", None)
            ada_group(9)
            v.wait_ge(S("ada_out"), 10)
            for b in range(4):
                filled("wout2", b, T_WQ)
                own(ttt(msv[:, b // 2, (b % 2) * 512:(b % 2 + 1) * 512], bank[b][:, :],
                        gate1[:, (b % 2) * 512:(b % 2 + 1) * 512], ALU.mult))
                own.sync()
                xv = xres[:, b // 2, (b % 2) * 512:(b % 2 + 1) * 512]
                ttt(xv, xv, msv[:, b // 2, (b % 2) * 512:(b % 2 + 1) * 512], ALU.add).then_inc(S("x3_done"), 1)
            scaled("wq", "n2")
            turned("wq_T", "wq", gain[:, 8:16], mod[:, 16:24])
            ada_group(10)
            ada_group(11)
            chunks(T_WQ, 16, pq, 0, S("pq_out"))

            for q in range(8):
                v.wait_ge(S("sc_mm"), q + 1)
                nc.vector.tensor_copy(scs[:, 4 * q:4 * q + 4, :], bank[q % 4][:, :].rearrange("p (a b) -> p a b", a=4))\
                    .then_inc(S("sc_out"), 1)
            LOWEST = -3.0e38

            def best16(vals, work, top_v, top_i, lists):
                for n in lists:
                    own(nc.vector.max(top_v[:, n, 0:8], vals[:, n, :]))
                own.sync()
                for n in lists:
                    own(nc.vector.max_index(top_i[:, n, 0:8].bitcast(U32), top_v[:, n, 0:8], vals[:, n, :]))
                    own(nc.vector.match_replace(work[:, n, :], top_v[:, n, 0:8], vals[:, n, :], LOWEST))
                own.sync()
                for n in lists:
                    own(nc.vector.max(top_v[:, n, 8:16], work[:, n, :]))
                own.sync()
                for n in lists:
                    own(nc.vector.max_index(top_i[:, n, 8:16].bitcast(U32), top_v[:, n, 8:16], work[:, n, :]))
                own.sync()

            v.wait_ge(S("sc_out"), 8)
            best16(scs, scr, pv, pI, range(32))
            own(nc.vector.tensor_copy(pIf, pI.bitcast(U32))); own.sync()
            v1, v2 = (pv.rearrange("p (l s) n -> p l s n", s=2)[:, :, s_2, :] for s_2 in range(2))
            i1, i2 = (pIf.rearrange("p (l s) n -> p l s n", s=2)[:, :, s_2, :] for s_2 in range(2))
            own(tsc(i1, i1, 128.0, None, ALU.mult)); own.sync()
            for a1, a2, dst in ((v1, v2, cand), (i1, i2, cidx)):
                for a in range(8):
                    n = 16 // (a + 1)
                    at = PAIRS.index((a, 0))
                    own(ttt(dst[:, :, at:at + n], a1[:, :, a:a + 1].to_broadcast([P, 16, n]), a2[:, :, 0:n], ALU.add))
                at = PAIRS.index((8, 0))
                own(ttt(dst[:, :, at:at + 8], a1[:, :, 8:16], a2[:, :, 0:1].to_broadcast([P, 16, 8]), ALU.add))
            own.sync()
            best16(cand, cand2, tv, tp, range(16))
            own(nc.vector.tensor_copy(tpf, tp.bitcast(U32)))
            ttt(tg, tv, tv[:, :, 0:1].to_broadcast([P, 16, 16]), ALU.subtract).then_inc(S("top_shift"), 1)
            own.sync()
            v.wait_ge(S("iota_in"), 16)
            for tt in range(TT):
                ls = slice(8 * tt, 8 * tt + 8)
                e4 = eqs.rearrange("p (l k) n -> p l k n", l=8)
                for l in range(8):
                    own(ttt(e4[:, l], tpf[:, 8 * tt + l, :].unsqueeze(2).to_broadcast([P, 16, NPAIR]),
                            iot[:, 0:NPAIR].unsqueeze(1).to_broadcast([P, 16, NPAIR]), ALU.is_equal))
                own.sync()
                for l in range(8):
                    own(ttt(e4[:, l], e4[:, l], cidx[:, 8 * tt + l, :].unsqueeze(1).to_broadcast([P, 16, NPAIR]),
                            ALU.mult))
                own.sync()
                own(nc.vector.tensor_reduce(tid[:, ls, :].rearrange("p a b -> p (a b)"), eqs, AX.X, ALU.add))
                own.sync()
            own(nc.vector.tensor_copy(tiu.bitcast(U32), tid)); own.sync()
            own(tsc(tp.bitcast(U32), tiu.bitcast(U32), 7, None, ALU.logical_shift_right))
            own(tsc(tiu.bitcast(U32), tiu.bitcast(U32), 127, None, ALU.bitwise_and)); own.sync()
            own(nc.vector.tensor_copy(t1f, tp.bitcast(U32)))
            own(nc.vector.tensor_copy(t2f, tiu.bitcast(U32)))
            v.wait_ge(S("top_exp"), 1)
            own(nc.vector.tensor_reduce(tsm, tg, AX.X, ALU.add)); own.sync()
            own(nc.vector.reciprocal(trs, tsm)); own.sync()
            ttt(tg, tg, trs.unsqueeze(2).to_broadcast([P, 16, 16]), ALU.mult).then_inc(S("chosen"), 1)
            v.wait_ge(S("chosen_T"), 1)
            own(nc.vector.tensor_copy(picks[:, 2, :], bank[7][:, 0:T])); own.sync()
            own(ttt(rest, bank[7][:, 0:T], picks[:, 2, :], ALU.subtract)); own.sync()
            own(nc.vector.tensor_copy(picks[:, 3, :], rest)); own.sync()
            own(ttt(picks[:, 4, :], rest, picks[:, 3, :], ALU.subtract)); own.sync()
            for j in range(2):
                nc.vector.tensor_copy(picks[:, j, :], bank[6][:, j * T:(j + 1) * T]).then_inc(S("weighted"), 1)
            v.wait_ge(S("weighted"), 2)

            def tokens(q, i):
                return slice(4 * q, 4 * q + 4) if i is None else bass.ds(i * 16 + 4 * q, 4)

            def onehots(half, q, i):
                k = (0 if i is None else i * R) + (HALF * half + q)
                if half or q >= 2:
                    v.wait_ge(S("weights_made"), k - 1)
                ts, slot = tokens(q, i), q % 2
                if half or q or i is not None:
                    v.wait_ge(S("onehot"), k)
                bc = lambda s_, n: picks[:, s_, ts].unsqueeze(2).to_broadcast([P, 4, n])
                ttt(same, bc(0, HALF), iot[:, HALF * half:HALF * (half + 1)].unsqueeze(1).to_broadcast([P, 4, HALF]),
                    ALU.is_equal).then_inc(S("same"), 1)
                ttt(oneB[:, slot], bc(1, P), iot.unsqueeze(1).to_broadcast([P, 4, P]), ALU.is_equal)
                v.wait_ge(S("same"), k + 1)
                ttt(oneA[:, slot], same.unsqueeze(1).to_broadcast([P, 3, 4, HALF]),
                    picks[:, 2:5, ts].unsqueeze(3).to_broadcast([P, 3, 4, HALF]), ALU.mult).then_inc(S("onehot"), 1)

            def weigh(half, q, i):
                k = (0 if i is None else i * R) + (HALF * half + q)
                v.wait_ge(S("weights_made"), k + 1)
                dst = units3[:, HALF * half:HALF * (half + 1), tokens(q, i)]
                ttt(dst, dst, bank[6 + q % 2][:, 0:4 * HALF].rearrange("p (t n) -> p n t", t=4), ALU.mult)\
                    .then_inc(S("weighted"), 1)

            def lower(c, i):
                k = 0 if i is None else i * R
                v.wait_ge(S("u_hi"), k + (c + 1))
                src = arena[:, c * T:(c + 1) * T] if i is None else arena[:, bass.ds(i * (R * T) + c * T, T)]
                ttt(ul[:, c % 2, :], src, uh[:, c % 2, :].bitcast(F32), ALU.subtract).then_inc(S("u_lo"), 1)

            for half in range(2):
                onehots(half, 0, None)
                v.wait_ge(S("expert_act"), HALF * (half + 1))
                if half:
                    lower(0, None)
                for q in range(1, R):
                    onehots(half, q, None)
                    if half:
                        lower(q, None)
                    weigh(half, q - 1, None)
                with v.Fori(0, HALF // R - 1) as i:
                    for u in range(R):
                        onehots(half, R + u, i)
                        if half:
                            lower(R + u, i)
                        weigh(half, R - 1 + u, i)
                weigh(half, HALF - 1, None)
            with v.Fori(0, HALF // R) as i:
                for u in range(R):
                    lower(HALF + u, i)
            v.wait_ge(S("last_in"), 48)
            for b in range(4):
                filled("peer", b, T_END)
                cs = slice((b % 2) * 512, (b % 2 + 1) * 512)
                own(ttt(fin_t[:, b // 2, cs], bank[b][:, :], fin_g[:, cs], ALU.mult)); own.sync()
                ttt(xres[:, b // 2, cs], xres[:, b // 2, cs], fin_t[:, b // 2, cs], ALU.add)\
                    .then_inc(S("x4_done"), 1)
            v.wait_ge(S("roots"), rooted("last"))
            for tt in range(TT):
                stt(fin_o[:, tt, :], xres[:, tt, :], rs("last", tt), fin_w, ALU.mult, ALU.mult)\
                    .then_inc(S("out_done"), 1)


def f_tiles(w):
    n = w.shape[1] // P
    return w.reshape(KC, P, n, P).transpose(2, 1, 0, 3).reshape(n, P, D)


def columns(v_):
    return v_.reshape(-1, P).T


def interleave(f, m):
    order = [f[0]]
    for i in range(len(f) - 1):
        order += [f[i + 1], m[i]]
    return order + [m[len(m) - 1]]


def kernel(**inputs):
    import concourse.bacc as bacc
    from concourse.bass_utils import run_bass_kernel_spmd

    a = {k: np.asarray(v_) for k, v_ in inputs.items()}
    w_in, w_in2 = a["w_in"][0], a["w_in_2"][0]
    at = np.cumsum([0, 512, 512, 1024, 1024, 16, 1024, 1024, 1024, 1024])
    q2, k2, v2, r2, alr, su, sv, ga, gb = (w_in2[:, at[j]:at[j + 1]] for j in range(9))
    tiles = list(f_tiles(np.concatenate([w_in[:, 0:1024], w_in[:, 1536:2560]], 1)))
    tiles += list(np.concatenate([w_in[:, 1024:1536], w_in[:, 2560:3072]], 1).reshape(KC, P, D))
    tiles += list(a["w_out"][0].reshape(KC, P, D))
    tiles += interleave(f_tiles(a["w_ff1"][0]), a["w_ff2"][0].reshape(N_FFN, P, D))
    tiles += list(f_tiles(np.concatenate([q2, k2], 1)))
    for w in (sv, su, v2, r2, ga, gb):
        tiles += list(w.reshape(KC, P, D))
    tiles += list(a["w_out_2"][0].reshape(KC, P, D))
    tiles += list(f_tiles(a["peer_w_q_2"][0]))
    down = a["peer_down_2"][0].reshape(N_PEER, P, KC, P).transpose(0, 3, 2, 1).reshape(N_PEER, P, D)
    tiles += list(down) + list(a["peer_up_2"][0].reshape(N_PEER, P, D))
    hg = a["hg_norm_w"][0]
    b_ada = a["b_ada_2"][0].reshape(6, D)
    w_ada = a["w_ada_2"][0].reshape(4, 2, P, 6, 2, 512)[:, :, :, [0, 1, 3, 4, 2, 5]]
    w_ada = w_ada.transpose(3, 4, 0, 2, 1, 5).reshape(N_ADA * P, D)
    cols = np.concatenate([
        columns(a["norm_mix"][0]), columns(a["norm_mlp"][0]), columns(a["norm1_w_2"][0]), columns(a["norm2_w_2"][0]),
        columns(np.concatenate([a["lru_out_norm"][0], hg, hg, hg, hg, a["att_out_norm"][0]])),
        columns(b_ada[[0, 1, 3, 4]].reshape(-1)), columns(a["c_2"][0]),
        a["lru_conv_w"][0].reshape(4, 2, P).transpose(2, 1, 0).reshape(P, 8), columns(a["lru_conv_b"][0]),
        columns(a["lru_ba"][0]), columns(a["lru_bx"][0]), columns(a["lru_lambda"][0]), columns(a["b_alpha_2"][0]),
        a["sgu_b_2"][0].T], 1)
    rows = np.concatenate([a["norm_final"], a["gla_norm_w_2"][0], a["sgu_ln_w_2"][0], a["sgu_ln_b_2"][0],
                           a["final_norm_w_2"], b_ada[2], b_ada[5]])[None]
    lru = [a[n][0].reshape(2, 2, 64, 64).transpose(1, 2, 0, 3).reshape(P, 128) for n in ("lru_wa", "lru_wx")]
    s, t = np.arange(P)[:, None], np.arange(P)[None, :]
    masks = [np.zeros((P, P), bool)]
    for h in LEVELS:
        masks.append((s // (2 * h) == t // (2 * h)) & (s % (2 * h) < h) & (t % (2 * h) >= h))
    rel = [np.where(k - q <= 0, k - q, -2.56e32) for q, k in
           ((np.arange(P)[:, None], np.arange(P)[None, :]), (P + np.arange(P)[:, None], np.arange(T)[None, :]))]
    arrays = {
        "x": a["x"][0].reshape(TT, P, D).transpose(1, 0, 2).reshape(P, TT * D),
        "stream": np.stack(tiles).reshape(T_END * P, D),
        "ada": w_ada,
        "cols": cols, "rows": rows, "lru_w": np.concatenate(lru, 1),
        "hgmask": np.concatenate(masks, 1).astype(np.uint32),
        "causal": (s <= t).astype(np.float32),
        "alibi": np.concatenate(rel, 1).astype(np.float32),
        "iota": np.concatenate([np.broadcast_to(t, (P, P)), np.eye(P)], 1).astype(np.float32),
        "walr": alr.reshape(KC, P, 16).transpose(1, 0, 2).reshape(P, P),
        "wup": a["w_alpha_up_2"][0],
        "sguw": a["sgu_w_2"][0].transpose(2, 0, 1).reshape(P, D),
        "keys": np.concatenate([a["peer_keys1_2"][0].T, a["peer_keys2_2"][0].T], 1),
    }
    nc = bacc.Bacc("TRN2", target_bir_lowering=False, num_devices=1)
    args = {}
    for name, v_ in arrays.items():
        arrays[name] = v_ = np.ascontiguousarray(v_)
        args[name] = nc.dram_tensor(name, v_.shape, mybir.dt.from_np(v_.dtype), kind="ExternalInput").ap()
    args["out"] = nc.dram_tensor("out", (T, D), F32, kind="ExternalOutput").ap()
    build(nc, **args)
    r = run_bass_kernel_spmd(nc, [arrays], core_ids=[0])
    return r.results[0]["out"].reshape(1, T, D)
```
